# Optimizing a Trainium2 kernel written in Bass

```python
import math
import jax, jax.numpy as jnp
from jax import lax
import numpy as np

D_MODEL = 1024
BATCH = 1
SEQ = 1024
DEPTH = 2

EPS = 1e-5
ATTN_HEADS = 8
ATTN_KV_HEADS = 2
HEAD_DIM = 64
WINDOW = 128
ATTN_BLOCK = 128
ATTN_WIDTH = ATTN_HEADS * HEAD_DIM
KV_WIDTH = ATTN_KV_HEADS * HEAD_DIM
POOL_WINDOWS = (2, 4, 8, 16)
POOL_GROUPS = 4
POOL_WIDTH = D_MODEL // 2
POOL_GROUP_DIM = POOL_WIDTH // POOL_GROUPS
AP_IN = ATTN_WIDTH + 2 * KV_WIDTH + POOL_WIDTH
AP_OUT = ATTN_WIDTH + POOL_WIDTH
SSD_INNER = 2 * D_MODEL
SSD_HEAD_DIM = 64
SSD_HEADS = SSD_INNER // SSD_HEAD_DIM
SSD_GROUPS = 4
SSD_STATE = 128
SSD_CONV = 4
SSD_CHUNK = 128
SSD_CONV_DIM = SSD_INNER + 2 * SSD_GROUPS * SSD_STATE
SSD_IN = 2 * SSD_INNER + 2 * SSD_GROUPS * SSD_STATE + SSD_HEADS
FFN_HIDDEN = -(-8 * D_MODEL // (3 * 256)) * 256
N_EVEN = (DEPTH + 1) // 2
N_ODD = DEPTH // 2

kernel_name = "hybrid_swa_sink_pool_ssd_trunk"

def rmsnorm(x, w):
    xf = x.astype(jnp.float32)
    y = xf * lax.rsqrt(jnp.mean(xf * xf, axis=-1, keepdims=True) + EPS) * w.astype(jnp.float32)
    return y.astype(x.dtype)

def sliding_window_attention(q, k, v, sinks):
    b, s = q.shape[0], q.shape[1]
    nb = s // ATTN_BLOCK
    g = ATTN_HEADS // ATTN_KV_HEADS
    qb = q.reshape(b, nb, ATTN_BLOCK, ATTN_KV_HEADS, g, HEAD_DIM)

    def band(t):
        tp = jnp.pad(t, ((0, 0), (ATTN_BLOCK, 0), (0, 0), (0, 0)))
        tp = tp.reshape(b, nb + 1, ATTN_BLOCK, ATTN_KV_HEADS, HEAD_DIM)
        return jnp.concatenate([tp[:, :-1], tp[:, 1:]], axis=2)

    kb, vb = band(k), band(v)
    scores = jnp.einsum('bnqhgd,bnkhd->bnhgqk', qb, kb).astype(jnp.float32) * (HEAD_DIM ** -0.5)
    n_idx = jnp.arange(nb)[:, None, None]
    qi = jnp.arange(ATTN_BLOCK)[None, :, None]
    kj = jnp.arange(2 * ATTN_BLOCK)[None, None, :]
    diff = qi + ATTN_BLOCK - kj
    k_pos = (n_idx - 1) * ATTN_BLOCK + kj
    mask = (diff >= 0) & (diff < WINDOW) & (k_pos >= 0)
    scores = jnp.where(mask[None, :, None, None], scores, -1e30)
    sink = sinks.astype(jnp.float32).reshape(ATTN_KV_HEADS, g)[None, None, :, :, None, None]
    sink = jnp.broadcast_to(sink, scores.shape[:-1] + (1,))
    probs = jax.nn.softmax(jnp.concatenate([scores, sink], axis=-1), axis=-1)[..., :-1]
    out = jnp.einsum('bnhgqk,bnkhd->bnqhgd', probs.astype(vb.dtype), vb)
    return out.reshape(b, s, ATTN_WIDTH)

def multiscale_pool(u, pool_w, pool_scale):
    b, s, _ = u.shape
    uf = u.astype(jnp.float32)
    count = jnp.arange(1, s + 1, dtype=jnp.float32)[:, None]
    outs = []
    for gi, w in enumerate(POOL_WINDOWS):
        ug = uf[..., gi * POOL_GROUP_DIM:(gi + 1) * POOL_GROUP_DIM]
        cs = jnp.cumsum(ug, axis=1)
        lower = jnp.pad(cs[:, :s - w], ((0, 0), (w, 0), (0, 0)))
        mean = (cs - lower) / jnp.minimum(count, float(w))
        outs.append(mean - ug)
    d = jnp.stack(outs, axis=2)
    y = jnp.einsum('bsgc,gcd->bsgd', d, pool_w.astype(jnp.float32)).reshape(b, s, POOL_WIDTH)
    return (y * pool_scale.astype(jnp.float32)).astype(u.dtype)

def attn_pool_mixer(u, w_in, sinks, pool_w, pool_scale, w_out):
    b, s, _ = u.shape
    proj = u @ w_in
    q = proj[..., :ATTN_WIDTH].reshape(b, s, ATTN_HEADS, HEAD_DIM)
    k = proj[..., ATTN_WIDTH:ATTN_WIDTH + KV_WIDTH].reshape(b, s, ATTN_KV_HEADS, HEAD_DIM)
    v = proj[..., ATTN_WIDTH + KV_WIDTH:ATTN_WIDTH + 2 * KV_WIDTH].reshape(b, s, ATTN_KV_HEADS, HEAD_DIM)
    p = proj[..., ATTN_WIDTH + 2 * KV_WIDTH:]
    a = sliding_window_attention(q, k, v, sinks)
    m = multiscale_pool(p, pool_w, pool_scale)
    return jnp.concatenate([a, m], axis=-1) @ w_out

def causal_depthwise_conv(x, w, bias):
    s = x.shape[1]
    xp = jnp.pad(x, ((0, 0), (SSD_CONV - 1, 0), (0, 0)))
    out = xp[:, 0:s] * w[0]
    for kk in range(1, SSD_CONV):
        out = out + xp[:, kk:kk + s] * w[kk]
    return out + bias

def ssd_chunked(x, dt, A, Bm, Cm):
    b, s, h, p = x.shape
    L = SSD_CHUNK
    nc = s // L
    G = SSD_GROUPS
    hg = h // G
    n = SSD_STATE
    xdt = (x.astype(jnp.float32) * dt[..., None]).reshape(b, nc, L, G, hg, p)
    Bc = Bm.astype(jnp.float32).reshape(b, nc, L, G, n)
    Cc = Cm.astype(jnp.float32).reshape(b, nc, L, G, n)
    dA = (dt * A).reshape(b, nc, L, G, hg)
    a_cs = jnp.moveaxis(jnp.cumsum(dA, axis=2), 2, -1)
    seg = a_cs[..., :, None] - a_cs[..., None, :]
    causal = jnp.tril(jnp.ones((L, L), dtype=bool))
    decay = jnp.exp(jnp.where(causal, seg, -jnp.inf))
    cb = jnp.einsum('bclgn,bcsgn->bcgls', Cc, Bc)
    y_diag = jnp.einsum('bcgls,bcghls,bcsghp->bclghp', cb, decay, xdt)
    decay_states = jnp.exp(a_cs[..., -1:] - a_cs)
    states = jnp.einsum('bclgn,bcghl,bclghp->bcghpn', Bc, decay_states, xdt)
    chunk_decay = jnp.exp(a_cs[..., -1])

    def step(hstate, inp):
        st, dec = inp
        return hstate * dec[..., None, None] + st, hstate

    h0 = jnp.zeros((b, G, hg, p, n), jnp.float32)
    _, prev = lax.scan(step, h0, (jnp.moveaxis(states, 1, 0), jnp.moveaxis(chunk_decay, 1, 0)))
    prev = jnp.moveaxis(prev, 0, 1)
    y_off = jnp.einsum('bclgn,bcghpn,bcghl->bclghp', Cc, prev, jnp.exp(a_cs))
    return (y_diag + y_off).reshape(b, s, h, p)

def ssd_mixer(u, w_in, conv_w, conv_b, dt_bias, A_log, D, norm_w, w_out):
    b, s, _ = u.shape
    proj = u @ w_in
    z = proj[..., :SSD_INNER]
    xbc = proj[..., SSD_INNER:SSD_INNER + SSD_CONV_DIM]
    dt_raw = proj[..., SSD_INNER + SSD_CONV_DIM:]
    xbc = jax.nn.silu(causal_depthwise_conv(xbc, conv_w, conv_b))
    gn = SSD_GROUPS * SSD_STATE
    xs = xbc[..., :SSD_INNER].reshape(b, s, SSD_HEADS, SSD_HEAD_DIM)
    Bm = xbc[..., SSD_INNER:SSD_INNER + gn].reshape(b, s, SSD_GROUPS, SSD_STATE)
    Cm = xbc[..., SSD_INNER + gn:].reshape(b, s, SSD_GROUPS, SSD_STATE)
    dt = jax.nn.softplus(dt_raw.astype(jnp.float32) + dt_bias.astype(jnp.float32))
    A = -jnp.exp(A_log.astype(jnp.float32))
    y = ssd_chunked(xs, dt, A, Bm, Cm) + xs.astype(jnp.float32) * D.astype(jnp.float32)[:, None]
    y = y.reshape(b, s, SSD_INNER) * jax.nn.silu(z.astype(jnp.float32))
    yg = y.reshape(b, s, SSD_GROUPS, SSD_INNER // SSD_GROUPS)
    yg = yg * lax.rsqrt(jnp.mean(yg * yg, axis=-1, keepdims=True) + EPS)
    y = yg.reshape(b, s, SSD_INNER) * norm_w.astype(jnp.float32)
    return y.astype(u.dtype) @ w_out

def swiglu(h, w_gate, w_up, w_down):
    return (jax.nn.silu(h @ w_gate) * (h @ w_up)) @ w_down

def setup_inputs(seed: int = 0) -> dict:
    key = jax.random.key(seed)
    ks = jax.random.split(key, 24)
    f32 = jnp.float32

    def nrm(k, shape, scale):
        return jax.random.normal(k, shape, f32) * scale

    x = jax.random.normal(ks[0], (BATCH, SEQ, D_MODEL), f32)
    mix_norm_w = 1.0 + nrm(ks[1], (DEPTH, D_MODEL), 0.1)
    ap_w_in = nrm(ks[2], (N_EVEN, D_MODEL, AP_IN), D_MODEL ** -0.5)
    ap_sinks = nrm(ks[3], (N_EVEN, ATTN_HEADS), 0.5)
    pool_w = nrm(ks[4], (N_EVEN, POOL_GROUPS, POOL_GROUP_DIM, POOL_GROUP_DIM), POOL_GROUP_DIM ** -0.5)
    pool_scale = 1.0 + nrm(ks[5], (N_EVEN, POOL_WIDTH), 0.1)
    ap_w_out = nrm(ks[6], (N_EVEN, AP_OUT, D_MODEL), AP_OUT ** -0.5)
    ssd_w_in = nrm(ks[7], (N_ODD, D_MODEL, SSD_IN), D_MODEL ** -0.5)
    ssd_conv_w = nrm(ks[8], (N_ODD, SSD_CONV, SSD_CONV_DIM), SSD_CONV ** -0.5)
    ssd_conv_b = nrm(ks[9], (N_ODD, SSD_CONV_DIM), 0.02)
    dt0 = jnp.exp(jax.random.uniform(ks[10], (N_ODD, SSD_HEADS), f32, math.log(1e-3), math.log(1e-1)))
    ssd_dt_bias = dt0 + jnp.log(-jnp.expm1(-dt0))
    ssd_A_log = jnp.log(jax.random.uniform(ks[11], (N_ODD, SSD_HEADS), f32, 1.0, 16.0))
    ssd_D = 1.0 + nrm(ks[12], (N_ODD, SSD_HEADS), 0.1)
    ssd_norm_w = 1.0 + nrm(ks[13], (N_ODD, SSD_INNER), 0.1)
    ssd_w_out = nrm(ks[14], (N_ODD, SSD_INNER, D_MODEL), SSD_INNER ** -0.5)
    ffn_norm_w = 1.0 + nrm(ks[15], (DEPTH, D_MODEL), 0.1)
    w_gate = nrm(ks[16], (DEPTH, D_MODEL, FFN_HIDDEN), D_MODEL ** -0.5)
    w_up = nrm(ks[17], (DEPTH, D_MODEL, FFN_HIDDEN), D_MODEL ** -0.5)
    w_down = nrm(ks[18], (DEPTH, FFN_HIDDEN, D_MODEL), FFN_HIDDEN ** -0.5)
    final_norm_w = 1.0 + nrm(ks[19], (D_MODEL,), 0.1)
    return {"x": x, "mix_norm_w": mix_norm_w, "ap_w_in": ap_w_in, "ap_sinks": ap_sinks,
            "pool_w": pool_w, "pool_scale": pool_scale, "ap_w_out": ap_w_out,
            "ssd_w_in": ssd_w_in, "ssd_conv_w": ssd_conv_w, "ssd_conv_b": ssd_conv_b,
            "ssd_dt_bias": ssd_dt_bias, "ssd_A_log": ssd_A_log, "ssd_D": ssd_D,
            "ssd_norm_w": ssd_norm_w, "ssd_w_out": ssd_w_out, "ffn_norm_w": ffn_norm_w,
            "w_gate": w_gate, "w_up": w_up, "w_down": w_down, "final_norm_w": final_norm_w}

def reference(x, mix_norm_w, ap_w_in, ap_sinks, pool_w, pool_scale, ap_w_out,
              ssd_w_in, ssd_conv_w, ssd_conv_b, ssd_dt_bias, ssd_A_log, ssd_D,
              ssd_norm_w, ssd_w_out, ffn_norm_w, w_gate, w_up, w_down, final_norm_w):
    for layer in range(DEPTH):
        i = layer // 2
        h = rmsnorm(x, mix_norm_w[layer])
        if layer % 2 == 0:
            x = x + attn_pool_mixer(h, ap_w_in[i], ap_sinks[i], pool_w[i], pool_scale[i], ap_w_out[i])
        else:
            x = x + ssd_mixer(h, ssd_w_in[i], ssd_conv_w[i], ssd_conv_b[i], ssd_dt_bias[i],
                              ssd_A_log[i], ssd_D[i], ssd_norm_w[i], ssd_w_out[i])
        h = rmsnorm(x, ffn_norm_w[layer])
        x = x + swiglu(h, w_gate[layer], w_up[layer], w_down[layer])
    return rmsnorm(x, final_norm_w)


_drawn_inputs = setup_inputs


def setup_inputs(seed=0):
    import zlib

    import numpy as np

    out = dict(_drawn_inputs(seed))
    spreads = {}
    factors = {'ap_sinks': 8.0, 'ssd_conv_b': 2.99}
    for name, (base, spread) in spreads.items():
        noise = np.random.default_rng([zlib.crc32(name.encode()), seed]).standard_normal(out[name].shape)
        drawn = base * np.exp(spread * noise) if base else spread * noise
        out[name] = __import__('jax').numpy.asarray(drawn.astype(out[name].dtype))
    for name, factor in factors.items():
        out[name] = (out[name] * factor).astype(out[name].dtype)
    return out
```

```python
from contextlib import ExitStack

import concourse.bass as bass
from concourse import mybir

F32 = mybir.dt.float32
F32R = mybir.dt.float32r
ALU = mybir.AluOpType
ACT = mybir.ActivationFunctionType
AX_X = mybir.AxisListType.X

P = 128
EPS = 1e-5
NEG = -1e30
WINDOWS = (2, 4, 8, 16)
KV_HEADS, HEADS, HEAD_DIM = 2, 8, 64
PAD = 16
RAW_SLOTS = 2
SPLIT_SLOTS = 6
LEAD = 4
BANK = 512


class Tally:

    def __init__(self, **starts):
        self.n = dict(starts)
        self.i, self.per, self.start = None, {}, {}

    def count(self, name, more=0):
        v = self.n[name] + more
        return v if self.i is None or not self.per.get(name) else self.i * self.per[name] + v

    def add(self, name, k=1):
        self.n[name] += k

    def enter(self, i, **per):
        self.i, self.per, self.start = i, per, dict(self.n)

    def leave(self, trips):
        for name, v in self.n.items():
            per = v - self.start[name]
            assert per == self.per.get(name, 0), (name, per)
            self.n[name] = self.start[name] + per * trips
        self.i = None


def trunk(nc, x, mix_norm_w, ap_w_in, ap_sinks, pool_w, pool_scale, ap_w_out, ssd_w_in, ssd_conv_w,
          ssd_conv_b, ssd_dt_bias, ssd_A_log, ssd_D, ssd_norm_w, ssd_w_out, ffn_norm_w, w_gate, w_up,
          w_down, final_norm_w, out):
    S, DM = x.shape[1], x.shape[2]
    NT = S // P
    NK = DM // P
    AW = HEADS * HEAD_DIM
    QH = HEADS // KV_HEADS
    FF = w_gate.shape[2]
    NF = FF // P
    FB = 2
    ROUNDS = NF // FB
    INNER = ssd_w_out.shape[1]
    SH = ssd_D.shape[1]
    PH = INNER // SH
    G = 4
    HG = SH // G
    BG = INNER // P // G
    CONV = ssd_conv_w.shape[1]
    CC = ssd_conv_w.shape[2]
    NCB = BG + 2
    assert S == NT * P == 1024 and DM == 1024 and NF == FB * ROUNDS and HG == 8 and BG == 4
    assert CONV == 4 and P == 128 and ap_w_in.shape[2] == AW + 2 * P + 4 * P

    GC_TAP, GC_BIAS = 0, NCB * CONV
    GC_D, GC_NW = GC_BIAS + NCB, GC_BIAS + NCB + BG
    GC_DT = GC_NW + BG
    GC_ACS, GC_DS, GC_CD = GC_DT + NT * HG, GC_DT + 2 * NT * HG, GC_DT + 3 * NT * HG
    GC = GC_DT + 4 * NT * HG

    ap_in = ap_w_in[0]
    pool_cols = [ap_in[:, AW + 2 * P + b * P:AW + 2 * P + (b + 1) * P].rearrange("(k p) c -> p k c", p=P)
                 for b in range(4)]
    kv_cols = [ap_in[:, AW + b * P:AW + (b + 1) * P].rearrange("(k p) c -> p k c", p=P) for b in range(2)]
    zc, xc = 0, INNER // P
    bc_, cc_ = xc + INNER // P, xc + INNER // P + G
    dtc = 2 * INNER + 2 * G * P

    with ExitStack() as ctx:
        def sb(name, shape, dt=F32):
            return ctx.enter_context(nc.sbuf_tensor(name, shape, dt))

        def sem(name):
            return ctx.enter_context(nc.semaphore(name))

        xres = sb("xres", [P, NT, DM])
        xn_hi = sb("xn_hi", [P, NK, S], F32R)
        xn_lo = sb("xn_lo", [P, NK, S], F32R)
        raw = [sb(f"w_raw{i}", [P, DM]) for i in range(RAW_SLOTS)]
        w_hi = [sb(f"w_hi{i}", [P, DM], F32R) for i in range(SPLIT_SLOTS)]
        w_lo = [sb(f"w_lo{i}", [P, DM], F32R) for i in range(SPLIT_SLOTS)]
        ident = sb("ident", [P, P])
        tri = sb("tri", [P, P], F32R)
        ones = sb("ones", [P, P], F32R)
        gconst = sb("gconst", [P, G, GC])
        gda_at = nc.sbuf_base
        gda_hi = sb("gda_hi", [P, G, NT * HG], F32R)
        gda_lo = sb("gda_lo", [P, G, NT * HG], F32R)
        gc = sb("gc", [P, GC])
        da_hi = sb("da_hi", [P, NT * HG], F32R)
        da_lo = sb("da_lo", [P, NT * HG], F32R)
        small = sb("small", [P, 176])
        eps = sb("eps", [P, 1])
        sink, dt_bias, exp_a, p_scale = small[:, 0:8], small[:, 8:40], small[:, 40:72], small[:, 72:76]
        ssq, std, rstd = small[:, 76:84], small[:, 84:92], small[:, 92:100]
        row_max, neg_max, row_sum, sink_exp = (
            [small[:, a + 4 * r:a + 4 * r + 4] for r in range(3)] for a in (100, 112, 124, 136))
        rms = small[:, 148:156]
        inv_count, one_col, neg_sink = small[:, 156:172], small[:, 172:173], sb("neg_sink", [P, 8])

        shared_at = nc.sbuf_base
        assert shared_at % 32 == 0 and gda_at % 32 == 0
        SHARED = 7 * S + 4 * S + P
        sb("shared", [P, SHARED])

        def at(name, start, shape, dt=F32, origin=shared_at):
            n = 1
            for d in shape:
                n *= d
            assert origin != shared_at or start + n <= SHARED
            return nc.alloc_sbuf_tensor_at(name, [P] + shape, dt, offset=origin + 4 * start)

        norm_w = at("norm_w", 0, [DM])
        masks = at("masks", 0, [2, 2 * P], origin=gda_at)
        stage = at("stage", 3072, [2, P])
        rep = at("rep", 3072 + 2 * P, [SH])
        qT = at("qT", 0, [4, S])
        kT = at("kT", 4 * S, [S + P])
        vt = at("vt", 4 * S + (S + P), [NT + 1, P])
        UO = 4 * S + 2 * (NT + 1) * P
        u = [at(f"u{b}", UO + b * (PAD + S), [PAD + S]) for b in range(4)]
        win = [at(f"win{i}", 4 * S + i * (S + P), [PAD + S]) for i in range(2)]
        pool_wt = at("pool_wt", UO + 4 * (PAD + S), [4, P])
        prob = [at(f"prob{r}", UO + r * 1024, [QH, 2 * P]) for r in range(3)]
        probT = at("probT", UO + 3 * 1024, [2, QH, P])
        h_hi = at("h_hi", 1024, [FB, S], F32R)
        h_lo = at("h_lo", 3072, [FB, S], F32R)
        gate = [at(f"gate{i}", 5120 + i * BANK, [BANK]) for i in range(2)]
        hid = [at(f"hid{i}", 6144 + i * BANK, [BANK]) for i in range(2)]
        xn = [at(f"xn{i}", 7168 + i * DM, [DM]) for i in range(2)]
        junk = at("junk", 9216, [DM])
        wdt = at("wdt", 10240, [NK, SH])
        wdt_hi = at("wdt_hi", 10496, [NK, SH], F32R)
        wdt_lo = at("wdt_lo", 10752, [NK, SH], F32R)
        D = [at(f"dtmp{i}", 2048 + i * 256, [NT, SH]) for i in range(8)]
        BT, CT = at("BT", 0, [S]), at("CT", 1024, [S])
        acc = [at(f"acc{i}", 2048 + i * 1024, [S]) for i in range(2)]
        mdec = at("mdec", 2048, [HG, P])
        xdt = [at(f"xdt{i}", 3072 + i * BANK, [HG * PH]) for i in range(2)]
        xds = at("xds", 4096, [HG * PH])
        btok = at("btok", 4608, [P])
        cbm = [at(f"cbm{i}", 4736 + i * P, [P]) for i in range(2)]
        eacs = [at(f"eacs{i}", 4992 + i * BANK, [BG, P]) for i in range(2)]
        state, decayed = at("state", 6016, [HG * PH]), at("decayed", 6528, [HG * PH])
        y_hi = at("y_hi", 0, [BG, S], F32R)
        sq = at("sq", 4 * S, [S])
        yx = at("yx", 7 * S, [BG, S])
        y_lo = at("y_lo", 7 * S, [BG, S], F32R)

        ps = ctx.enter_context(nc.psum_tensor("ps", [P, 8, BANK], F32))

        BC_BANKS = (0, 1, 6)

        def pair(n):
            return ps[:, 2 * (n % 2):2 * (n % 2) + 2, :]

        def flat(ap):
            return ap.rearrange("p a b -> p (a b)")

        def f(ap):
            return ap.bitcast(F32)

        NA = 18
        RP, GP = 3 * FB, NCB + 2 * BG
        ssd_slots = [0, 1, 2, 3, 4, 5, 0, 1, 2, 3, 4, 5, 2, 3]
        seq = [(n % SPLIT_SLOTS, n % RAW_SLOTS) for n in range(NA)]
        for layer in range(2):
            FFN0 = len(seq)
            seq += [(n % SPLIT_SLOTS, n % RAW_SLOTS) for _ in range(ROUNDS) for n in range(RP)]
            if layer == 0:
                SSD0 = len(seq)
                seq += [(s, n % RAW_SLOTS) for _ in range(G) for n, s in enumerate(ssd_slots)]
        FFN_AT = (NA, FFN0)
        halves = set(range(4, 8)) | set(range(14, 18))

        class Piece:

            def __init__(self, n, i=None, per=0, turns=1):
                self.n, self.i, self.per = n, i, per
                all_ = [n + t * per for t in range(turns)]
                self.slot, self.raw = seq[n]
                assert all(seq[m] == seq[n] for m in all_)

                def back(m, which):
                    return next((d for d in range(1, m + 1) if seq[m - d][which] == seq[m][which]), None)

                def least(which):
                    got = [back(m, which) for m in all_]
                    return None if got[0] is None else min(got)
                self.slot_back, self.raw_back = least(0), least(1)

                def parts(m):
                    return sum(2 if k in halves else 1 for k in range(m + 1) if seq[k][1] == self.raw)
                self.parts = parts(n)
                self.parts_per = parts(n + per) - parts(n) if turns > 1 else 0

            def count(self, more=0):
                return self.n + more if self.i is None else self.i * self.per + (self.n + more)

            def raw_count(self):
                return 16 * self.parts if self.i is None else self.i * (16 * self.parts_per) + 16 * self.parts

        raw_ready = [sem(f"raw_ready{i}") for i in range(RAW_SLOTS)]
        hi_done, lo_done = sem("hi_done"), sem("lo_done")
        pair_full = sem("pair_full")
        pair_freed = sem("pair_freed")
        out_full = sem("out_full")
        out_added = sem("out_added")
        x_loaded = [sem(f"x_loaded{t}") for t in range(NT)]
        norm_w_loaded, const_loaded, wdt_loaded = sem("norm_w_loaded"), sem("const_loaded"), sem("wdt_loaded")
        masks_ready = sem("masks_ready")
        const_T, const_ready = sem("const_T"), sem("const_ready")
        ssq_ready, std_ready = sem("ssq_ready"), sem("std_ready")
        rstd_ready, xn_ready = sem("rstd_ready"), sem("xn_ready")
        xn_hi_done = sem("xn_hi_done")
        step_done = sem("step_done")
        d_ready = sem("d_ready")
        cat_hi_done, cat_done = sem("cat_hi_done"), sem("cat_done")
        max_ready, p_ready = sem("max_ready"), sem("p_ready")
        rsum_ready, p_normed = sem("rsum_ready"), sem("p_normed")
        t_full, pT_ready = sem("t_full"), sem("pT_ready")
        v_full, po_full, po_added = sem("v_full"), sem("po_full"), sem("po_added")
        gate_done = sem("gate_done")
        h_hi_done, h_split = sem("h_hi_done"), sem("h_split")
        wdt_hi_done, wdt_split = sem("wdt_hi_done"), sem("wdt_split")
        dts_v, dts_a = sem("dts_v"), sem("dts_a")
        gc_ready = sem("gc_ready")
        acc_ready, silu_done = sem("acc_ready"), sem("silu_done")
        cb_full, xsT_full, bc_full = sem("cb_full"), sem("xsT_full"), sem("bc_full")
        cb_freed, xdt_ready, m_ready = sem("cb_freed"), sem("xdt_ready"), sem("m_ready")
        relu_done, dec_ready, e_ready = sem("relu_done"), sem("dec_ready"), sem("e_ready")
        xds_ready, decayed_ready = sem("xds_ready"), sem("decayed_ready")
        state_ready = sem("state_ready")
        states_full, yoff_full, ydiag_full = sem("states_full"), sem("yoff_full"), sem("ydiag_full")
        yoff_read, y_ready = sem("yoff_read"), sem("y_ready")
        z_done, sq_ready, y_hi_done = sem("z_done"), sem("sq_ready"), sem("y_hi_done")
        y_split = sem("y_split")
        ssq_full, ssq_sum, rms_rooted, rms_ready = sem("ssq_full"), sem("ssq_sum"), sem("rms_rooted"), sem("rms_ready")
        final_ready = sem("final_ready")
        stored = [sem("stored0"), sem("stored1")]

        block = ctx.enter_context(nc.Block())

        @block.sync
        def _(sp):
            def load(piece, *srcs):
                if piece.raw_back is not None:
                    sp.wait_ge(lo_done, piece.count(1 - piece.raw_back))
                dst = raw[piece.raw]
                if len(srcs) == 2 and srcs[0].shape[0] == P:
                    v = dst[:, :].rearrange("p (k c) -> p k c", c=P)
                    for h, s in enumerate(srcs):
                        sp.dma_start(v[:, :, h * HEAD_DIM:(h + 1) * HEAD_DIM], s).then_inc(raw_ready[piece.raw], 16)
                elif len(srcs) == 2:
                    for h, s in enumerate(srcs):
                        sp.dma_start(dst[h * HEAD_DIM:(h + 1) * HEAD_DIM, :], s).then_inc(raw_ready[piece.raw], 16)
                else:
                    s = srcs[0]
                    d = dst[:, :] if len(s.shape) == 2 else dst[:, :].rearrange("p (k c) -> p k c", c=P)
                    sp.dma_start(d, s).then_inc(raw_ready[piece.raw], 16)

            def q_half(h):
                return ap_in[:, h * HEAD_DIM:(h + 1) * HEAD_DIM].rearrange("(k p) c -> p k c", p=P)
            srcs = [(c,) for c in pool_cols]
            srcs += [(q_half(i), q_half(i + 4)) for i in range(4)] + [(c,) for c in kv_cols]
            srcs += [(ap_w_out[0, AW + b * P:AW + (b + 1) * P, :],) for b in range(4)]
            srcs += [tuple(ap_w_out[0, h * HEAD_DIM:(h + 1) * HEAD_DIM, :] for h in (i, i + 4)) for i in range(4)]
            for n, s in enumerate(srcs):
                load(Piece(n), *s)

            def ffn(layer):
                wg, wu, wd = w_gate[layer], w_up[layer], w_down[layer]
                rows = wd.rearrange("(j p) n -> p j n", p=P)
                with sp.Fori(0, ROUNDS) as i:
                    for b in range(FB):
                        for m, w in enumerate((wg, wu)):
                            blk = w.rearrange("(k p) (j c) -> p k j c", p=P, c=P)[:, :, bass.ds(i * FB + b, 1), :]
                            load(Piece(FFN_AT[layer] + 2 * b + m, i, RP, ROUNDS), blk.rearrange("p k j c -> p k (j c)"))
                    for b in range(FB):
                        blk = rows[:, bass.ds(i * FB + b, 1), :]
                        load(Piece(FFN_AT[layer] + 4 + b, i, RP, ROUNDS), blk.rearrange("p j n -> p (j n)"))

            ffn(0)
            w_in = ssd_w_in[0]
            blocks = w_in[:, 0:(dtc // P) * P].rearrange("(k p) (j c) -> p k j c", p=P, c=P)
            rows = ssd_w_out[0].rearrange("(j p) n -> p j n", p=P)
            with sp.Fori(0, G) as g:
                firsts = [g + bc_, g + cc_] + [g * BG + xc + b for b in range(BG)] + [g * BG + zc + b for b in range(BG)]
                for k, j in enumerate(firsts):
                    load(Piece(SSD0 + k, g, GP, G), blocks[:, :, bass.ds(j, 1), :].rearrange("p k j c -> p k (j c)"))
                for b in range(BG):
                    load(Piece(SSD0 + NCB + BG + b, g, GP, G),
                         rows[:, bass.ds(g * BG + b, 1), :].rearrange("p j n -> p (j n)"))
            ffn(1)

        @block.gpsimd
        def _(pool):
            pool.memset(ident[:, :], 0.0).then_inc(masks_ready, 1)
            pool.memset(f(tri[:, :]), 1.0).then_inc(masks_ready, 1)
            pool.memset(f(ones[:, :]), 1.0).then_inc(masks_ready, 1)
            pool.memset(masks[:, 1, :], 0.0).then_inc(masks_ready, 1)
            pool.memset(masks[:, 0, P:2 * P], 0.0).then_inc(masks_ready, 1)
            pool.memset(one_col, 1.0).then_inc(masks_ready, 1)
            pool.memset(eps[:, :], EPS).then_inc(masks_ready, 1)
            pool.memset(masks[:, 0, 0:P], NEG).then_inc(masks_ready, 1)
            for j in range(PAD):
                pool.memset(inv_count[:, j:j + 1], 1.0 / (j + 1)).then_inc(masks_ready, 1)
            pool.wait_ge(masks_ready, 8 + PAD)
            pool.affine_select(out=ident[:, :], in_=ident[:, :], compare_op=ALU.not_equal, fill=1.0, base=0,
                               pattern=[[-1, P]], channel_multiplier=1).then_inc(masks_ready, 1)
            pool.affine_select(out=tri[:, :], in_=f(tri[:, :]), compare_op=ALU.is_ge, fill=0.0, base=0,
                               pattern=[[1, P]], channel_multiplier=-1).then_inc(masks_ready, 1)
            pool.affine_select(out=masks[:, 1, 0:P], in_=masks[:, 1, 0:P], compare_op=ALU.is_ge, fill=NEG, base=-1,
                               pattern=[[1, P]], channel_multiplier=-1).then_inc(masks_ready, 1)
            for m in range(2):
                pool.affine_select(out=masks[:, m, P:2 * P], in_=masks[:, m, P:2 * P], compare_op=ALU.is_ge, fill=NEG,
                                   base=0, pattern=[[-1, P]], channel_multiplier=1).then_inc(masks_ready, 1)

            def lo(piece):
                pool.wait_ge(hi_done, piece.count(1))
                pool.tensor_tensor(w_lo[piece.slot][:, :], raw[piece.raw][:, :], f(w_hi[piece.slot][:, :]),
                                   ALU.subtract).then_inc(lo_done, 1)

            for n in range(10 + LEAD + 2):
                lo(Piece(n))

            for j in range(2 * NT):
                pool.wait_ge(rsum_ready, j + 1)
                pr = prob[j % 3]
                pool.tensor_tensor(pr[:, :, :], pr[:, :, :],
                                   row_sum[j % 3].unsqueeze(2).to_broadcast([P, QH, 2 * P]), ALU.mult)\
                    .then_inc(p_normed, 1)
            for n in range(10 + LEAD + 2, NA):
                lo(Piece(n))

            def ffn(layer):
                with pool.Fori(0, ROUNDS) as i:
                    for k in range(RP):
                        lo(Piece(FFN_AT[layer] + k, i, RP, ROUNDS))

            ffn(0)
            pool.wait_ge(wdt_hi_done, 1)
            pool.tensor_tensor(wdt_lo[:, :, :], wdt[:, :, :], f(wdt_hi[:, :, :]), ALU.subtract).then_inc(wdt_split, 1)
            with pool.Fori(0, G) as g:
                for k in range(NCB + LEAD):
                    lo(Piece(SSD0 + k, g, GP, G))
                for c in range(NT):
                    def heads(ap):
                        return ap[:, :].rearrange("p (h d) -> p h d", d=PH)

                    def factor(first):
                        return gc[:, first + c * HG:first + (c + 1) * HG].unsqueeze(2).to_broadcast([P, HG, PH])
                    pool.wait_ge(xdt_ready, g * NT + (c + 1))
                    if c:
                        pool.wait_ge(states_full, g * NT + c)
                    pool.tensor_tensor(heads(xds), heads(xdt[c % 2]), factor(GC_DS), ALU.mult).then_inc(xds_ready, 1)
                    if c:
                        pool.wait_ge(state_ready, g * NT + c)
                        pool.tensor_tensor(heads(decayed), heads(state), factor(GC_CD), ALU.mult)\
                            .then_inc(decayed_ready, 1)
                for k in range(NCB + LEAD, GP):
                    lo(Piece(SSD0 + k, g, GP, G))
            ffn(1)

        @block.scalar
        def _(act):
            def load_norm_w(w):
                act.dma_start(norm_w[:, :], w.rearrange("(a n) -> a n", a=1).to_broadcast([P, DM]))\
                    .then_inc(norm_w_loaded, 16)

            load_norm_w(mix_norm_w[0])
            for tt in range(NT):
                act.dma_start(xres[:, tt, :], x[0, tt * P:(tt + 1) * P, :]).then_inc(x_loaded[tt], 16)
            NB = CC // P
            for dst, src in ((stage[0:CONV * NB, 0, :], ssd_conv_w[0].rearrange("t (b p) -> (t b) p", p=P)),
                             (stage[CONV * NB:(CONV + 1) * NB, 0, :], ssd_conv_b[0].rearrange("(b p) -> b p", p=P)),
                             (stage[0:G * BG, 1, :], ssd_norm_w[0].rearrange("(b p) -> b p", p=P)),
                             (stage[G * BG:G * BG + 4, 1, :], pool_scale[0].rearrange("(b p) -> b p", p=P)),
                             (sink, ap_sinks.to_broadcast([P, HEADS])), (dt_bias, ssd_dt_bias.to_broadcast([P, SH])),
                             (exp_a, ssd_A_log.to_broadcast([P, SH])), (rep[:, :], ssd_D.to_broadcast([P, SH])),
                             (pool_wt[:, :, :], pool_w[0].rearrange("g c d -> c g d"))):
                act.dma_start(dst, src).then_inc(const_loaded, 16)

            t = Tally(unit=0, out=0, tile=0, chunk=0, half=0, conv=0, z=0, gu=0)

            def hi(piece, free=None, count=None):
                if free is not None:
                    act.wait_ge(free, count)
                act.wait_ge(raw_ready[piece.raw], piece.raw_count())
                act.activation(w_hi[piece.slot][:, :], raw[piece.raw][:, :], ACT.Copy).then_inc(hi_done, 1)

            def square(tt):
                act.activation(junk[:, :], xres[:, tt, :], ACT.Square, accum_out=ssq[:, tt:tt + 1]).then_inc(ssq_ready, 1)
                t.add("tile")
                act.wait_ge(ssq_ready, t.count("tile"))
                act.activation(std[:, tt:tt + 1], ssq[:, tt:tt + 1], ACT.Sqrt, scale=1.0 / DM, bias=eps[:, :])\
                    .then_inc(std_ready, 1)

            def norm(wait_tile):
                unit0 = t.n["unit"]

                def xhi(tt):
                    act.wait_ge(pair_full, unit0 + tt + 1)
                    act.activation(xn_hi[:, :, tt * P:(tt + 1) * P],
                                   pair(unit0 + tt).rearrange("p a (b c) -> p (a b) c", c=P), ACT.Copy)\
                        .then_inc(xn_hi_done, 1)
                for tt in range(NT):
                    wait_tile(tt)
                    square(tt)
                    if tt >= 3:
                        xhi(tt - 3)
                for tt in range(NT - 3, NT):
                    xhi(tt)
                t.add("unit", NT)

            act.wait_ge(masks_ready, PAD + 13)
            for n in range(LEAD):
                hi(Piece(n))
            norm(lambda tt: act.wait_ge(x_loaded[tt], 16))

            for k in range(10):
                t.add("unit")
                hi(Piece(k + LEAD), pair_full, t.count("unit"))
            for n in (10 + LEAD, 11 + LEAD):
                hi(Piece(n))

            act.wait_ge(const_ready, 1)
            for b in range(4):
                act.wait_ge(pair_full, t.count("unit", 1))
                act.activation(xn_hi[:, 4 + b, :], flat(pair(t.n["unit"])), ACT.Copy, scale=p_scale[:, b:b + 1])\
                    .then_inc(cat_hi_done, 1)
                t.add("unit")

            NJ = 2 * NT

            def exps(j):
                act.wait_ge(max_ready, j + 1)
                r = j % 3
                for h in range(QH):
                    act.activation(prob[r][:, h, :], prob[r][:, h, :], ACT.Exp, bias=neg_max[r][:, h:h + 1],
                                   accum_out=row_sum[r][:, h:h + 1])
                act.activation(sink_exp[r], sink_exp[r], ACT.Exp).then_inc(p_ready, 1)

            def v_hi(j):
                rows = slice(64 * (j % 2), 64 * (j % 2) + 64)
                act.wait_ge(v_full, j + 1)
                act.activation(xn_hi[rows, 0:QH, (j // 2) * P:(j // 2 + 1) * P],
                               ps[rows, 6, :].rearrange("p (h q) -> p h q", q=P), ACT.Copy).then_inc(cat_hi_done, 1)

            exps(0)
            exps(1)
            for j in range(NJ):
                if j >= 1:
                    v_hi(j - 1)
                if j + 2 < NJ:
                    exps(j + 2)
                act.wait_ge(t_full, j + 1)
                act.activation(probT[:, :, :, :].rearrange("p a b c -> p (a b c)"),
                               ps[:, 4:6, :].rearrange("p a b -> p (a b)"), ACT.Copy).then_inc(pT_ready, 1)
            v_hi(NJ - 1)
            t.add("unit", NJ)
            load_norm_w(ffn_norm_w[0])
            for n in range(12 + LEAD, NA + 2):
                hi(Piece(n), po_full, NJ)

            def norm_after_outs():
                o = t.n["out"]
                norm(lambda tt: act.wait_ge(out_added, o + 2 * tt + 2))
                t.add("out", 2 * NT)

            norm_after_outs()
            for n in (NA + 2, NA + 3):
                hi(Piece(n))

            def gate_up(n0, i, turns):
                for b in range(FB):
                    hi(Piece(n0 + 4 + b, i, RP, turns), out_full, t.count("out"))
                for k in range(2 * FB):
                    act.wait_ge(pair_full, t.count("unit", 1))
                    act.activation(gate[k % 2][:, :], pair(t.n["unit"])[:, 0, :], ACT.Silu).then_inc(gate_done, 1)
                    act.wait_ge(pair_freed, t.count("unit", 1))
                    act.activation(h_hi[:, k // 2, (k % 2) * BANK:(k % 2 + 1) * BANK], hid[k % 2][:, :], ACT.Copy)\
                        .then_inc(h_hi_done, 1)
                    t.add("gu")
                    t.add("unit")

            def ffn(layer):
                n0 = FFN_AT[layer]
                gate_up(n0, None, 1)
                with act.Fori(0, ROUNDS - 1) as i:
                    t.enter(i, unit=2 * FB, gu=2 * FB, out=2 * NT)
                    for k in range(LEAD):
                        hi(Piece(n0 + RP + k, i, RP, ROUNDS - 1))
                    t.add("out", 2 * NT)
                    gate_up(n0 + RP, i, ROUNDS - 1)
                    t.leave(ROUNDS - 1)

            act.wait_ge(xn_ready, 2 * NT)
            load_norm_w(mix_norm_w[1])
            act.dma_start(wdt[:, :, :], ssd_w_in[0][:, dtc:dtc + SH].rearrange("(k p) c -> p k c", p=P))\
                .then_inc(wdt_loaded, 16)
            ffn(0)
            act.wait_ge(wdt_loaded, 16)
            act.activation(wdt_hi[:, :, :], wdt[:, :, :], ACT.Copy).then_inc(wdt_hi_done, 1)
            for k in range(LEAD):
                hi(Piece(SSD0 + k))
            norm_after_outs()

            act.wait_ge(dts_v, 1)
            act.activation(D[2][:, :, :], D[1][:, :, :], ACT.Exp, scale=-1.0).then_inc(dts_a, 1)
            act.activation(exp_a, exp_a, ACT.Exp).then_inc(dts_a, 1)
            act.wait_ge(dts_v, 2)
            act.activation(D[4][:, :, :], D[3][:, :, :], ACT.Ln).then_inc(dts_a, 1)
            act.wait_ge(dts_v, 3)
            act.activation(gda_hi[:, :, :].rearrange("p g (c h) -> p g c h", h=HG),
                           D[6][:, :, :].rearrange("p c (g h) -> p g c h", h=HG), ACT.Copy).then_inc(dts_a, 1)
            act.wait_ge(dts_v, 5)
            for d, first in ((D[3], GC_DS), (D[7], GC_CD)):
                act.activation(gconst[:, :, first:first + NT * HG],
                               d[:, :, :].rearrange("p c s -> p (c s)").rearrange("p (g k) -> p g k", g=G), ACT.Exp)\
                    .then_inc(dts_a, 1)
            t.add("unit", 2)

            with act.Fori(0, G) as g:
                t.enter(g, unit=NCB + BG, conv=NCB, z=BG, chunk=NT, half=2 * NT, out=2 * NT)
                act.wait_ge(gc_ready, g + 1)
                for k in range(NCB):
                    act.wait_ge(pair_full, t.count("unit", 1))
                    act.activation(acc[k % 2][:, :], flat(pair(t.n["unit"])), ACT.Identity,
                                   scale=gc[:, GC_TAP + k * CONV + CONV - 1:GC_TAP + k * CONV + CONV],
                                   bias=gc[:, GC_BIAS + k:GC_BIAS + k + 1]).then_inc(acc_ready, 1)
                    hi(Piece(SSD0 + LEAD + k, g, GP, G))
                    act.wait_ge(pair_freed, t.count("unit", 1))
                    dst = (BT[:, :], CT[:, :])[k] if k < 2 else yx[:, k - 2, :]
                    act.activation(dst, acc[k % 2][:, :], ACT.Silu).then_inc(silu_done, 1)
                    t.add("unit")
                    t.add("conv")
                for c in range(NT):
                    for hf in range(2):
                        act.wait_ge(bc_full, t.count("half", 1))
                        bc = ps[:, BC_BANKS[(2 * c + hf) % 3], :].rearrange("p (h l) -> p h l", l=P)
                        if hf == 0 and c >= 2:
                            act.wait_ge(y_ready, t.count("chunk", -1))
                        for odd in range(2):
                            rows = slice(64 * odd, 64 * odd + 64)
                            ins = act.activation(eacs[c % 2][rows, 2 * hf:2 * hf + 2, :], bc[rows, odd::2, :], ACT.Exp)
                        ins.then_inc(e_ready, 1)
                        act.wait_ge(e_ready, t.count("half", 1))
                        for h in range(4):
                            col = GC_ACS + c * HG + 4 * hf + h
                            ins = act.activation(bc[:, h, :], bc[:, h, :], ACT.Relu, scale=-1.0, bias=gc[:, col:col + 1])
                        ins.then_inc(relu_done, 1)
                        t.add("half")
                        act.wait_ge(relu_done, t.count("half"))
                        act.activation(bc, bc, ACT.Exp, scale=-1.0).then_inc(dec_ready, 1)
                    t.add("chunk")
                for k in range(BG):
                    act.wait_ge(pair_full, t.count("unit", 1))
                    pz = flat(pair(t.n["unit"]))
                    act.activation(pz, pz, ACT.Silu).then_inc(z_done, 1)
                    hi(Piece(SSD0 + LEAD + NCB + k, g, GP, G))
                    act.wait_ge(pair_freed, t.count("unit", 1))
                    if k:
                        act.wait_ge(ssq_full, t.count("z"))
                    act.activation(sq[:, :], yx[:, k, :], ACT.Square).then_inc(sq_ready, 1)
                    act.activation(y_hi[:, k, :], yx[:, k, :], ACT.Copy, scale=gc[:, GC_NW + k:GC_NW + k + 1])\
                        .then_inc(y_hi_done, 1)
                    t.add("unit")
                    t.add("z")
                act.wait_ge(ssq_sum, g + 1)
                act.activation(rms, rms, ACT.Sqrt, scale=1.0 / (BG * P), bias=eps[:, :]).then_inc(rms_rooted, 1)
                t.add("out", 2 * NT)
                for k in range(LEAD):
                    free = (out_full, t.count("out")) if k >= 2 else ()
                    hi(Piece(SSD0 + GP + k, g, GP, G), *free)
                t.leave(G)
            load_norm_w(ffn_norm_w[1])
            all_added = t.n["out"]
            norm(lambda tt: act.wait_ge(out_added, all_added))

            act.wait_ge(xn_ready, 4 * NT)
            load_norm_w(final_norm_w)
            ffn(1)
            o = t.n["out"]

            def store(tt):
                act.wait_ge(final_ready, tt + 1)
                act.dma_start(out[0, tt * P:(tt + 1) * P, :], xn[tt % 2][:, :]).then_inc(stored[tt % 2], 16)
            for tt in range(NT):
                act.wait_ge(out_added, o + 2 * tt + 2)
                square(tt)
                if tt:
                    store(tt - 1)
            store(NT - 1)
            for i in range(2):
                act.wait_ge(stored[i], 16 * NT // 2)

        @block.tensor
        def _(pe):
            t = Tally(unit=0, out=0, tile=0, conv=0, z=0, gu=0, chunk=0, half=0)

            def mm3(dst, l_hi, l_lo, r_hi, r_lo, first, last):
                pe.matmul(dst, l_hi, r_hi, start=first, stop=False)
                pe.matmul(dst, l_hi, r_lo, start=False, stop=False)
                return pe.matmul(dst, l_lo, r_hi, start=False, stop=last)

            def begin_unit():
                if t.i is not None or t.n["unit"] >= 2:
                    pe.wait_ge(pair_freed, t.count("unit", -1))
                p = pair(t.n["unit"])
                t.add("unit")
                return p

            def begin_out():
                if t.i is not None or t.n["out"] >= 4:
                    pe.wait_ge(out_added, t.count("out", -3))
                bank = ps[:, 4 + t.n["out"] % 4, :]
                t.add("out")
                return bank

            def norm_T(tt):
                pe.wait_ge(xn_ready, t.count("tile", 1))
                p = begin_unit().rearrange("p a (b c) -> p (a b) c", c=P)
                for k in range(NK):
                    ins = pe.transpose(p[:, k, :], xn[tt % 2][:, k * P:(k + 1) * P], ident[:, :])
                ins.then_inc(pair_full, 1)
                t.add("tile")

            def split_of(piece):
                return [w[piece.slot][:, :].rearrange("p (k c) -> p k c", c=P) for w in (w_hi, w_lo)]

            def columns(dst, piece, half):
                p_hi, p_lo = split_of(piece)
                tok = slice(half * BANK, (half + 1) * BANK)
                for k in range(NK):
                    ins = mm3(dst, p_hi[:, k, :], p_lo[:, k, :], xn_hi[:, k, tok], xn_lo[:, k, tok],
                              k == 0, k == NK - 1)
                return ins

            def project(piece):
                pe.wait_ge(lo_done, piece.count(1))
                p = begin_unit()
                columns(p[:, 0, :], piece, 0)
                columns(p[:, 1, :], piece, 1).then_inc(pair_full, 1)

            def rows(bank, n, parts):
                tok, col = slice(n // 2 * P, (n // 2 + 1) * P), slice(n % 2 * BANK, (n % 2 + 1) * BANK)
                for k, (a_hi, a_lo, slot) in enumerate(parts):
                    ins = mm3(bank, a_hi[:, tok], a_lo[:, tok], w_hi[slot][:, col], w_lo[slot][:, col],
                              k == 0, k == len(parts) - 1)
                return ins

            def outputs(parts, with_norm=False, before=None):
                for n in range(2 * NT):
                    if before:
                        before(n)
                    rows(begin_out(), n, parts).then_inc(out_full, 1)
                    if with_norm and n % 2 and n // 2 >= 2:
                        norm_T(n // 2 - 2)
                if with_norm:
                    norm_T(NT - 2)
                    norm_T(NT - 1)

            pe.wait_ge(masks_ready, 13 + PAD)
            for tt in range(NT):
                norm_T(tt)
            pe.wait_ge(const_loaded, 16 * 9)
            NB = CC // P
            pe.transpose(ps[:, 4, 0:(CONV + 1) * NB], stage[0:(CONV + 1) * NB, 0, :], ident[0:(CONV + 1) * NB, 0:(CONV + 1) * NB])
            pe.transpose(ps[:, 4, P:P + G * BG + 4], stage[0:G * BG + 4, 1, :], ident[0:G * BG + 4, 0:G * BG + 4])\
                .then_inc(const_T, 1)
            pe.wait_ge(pair_freed, NT)

            for k in range(9):
                project(Piece(k))
            pe.wait_ge(lo_done, 10)
            p = begin_unit().rearrange("p a (b c) -> p (a b) c", c=P)
            v_hi, v_lo = split_of(Piece(9))
            for tt in range(NT):
                tok = slice(tt * P, (tt + 1) * P)
                for k in range(NK):
                    ins = mm3(p[:, tt, :], xn_hi[:, k, tok], xn_lo[:, k, tok], v_hi[:, k, :], v_lo[:, k, :],
                              k == 0, k == NK - 1)
            ins.then_inc(pair_full, 1)

            pe.wait_ge(d_ready, 4)
            for b in range(4):
                p = begin_unit()
                for half in range(2):
                    ins = pe.matmul(p[:, half, :], pool_wt[:, b, :], u[b][:, PAD + half * BANK:PAD + (half + 1) * BANK],
                                    start=True, stop=True)
                ins.then_inc(pair_full, 1)

            NJ = 2 * NT

            def scores(j):
                n, kv = j // 2, j % 2
                hd = slice(64 * kv, 64 * kv + 64)
                p = begin_unit().rearrange("p a (b c) -> p (a b) c", c=2 * P)
                for h in range(QH):
                    ins = pe.matmul(p[:, h, :], qT[hd, h, n * P:(n + 1) * P], kT[hd, n * P:(n + 2) * P],
                                    start=True, stop=True)
                ins.then_inc(pair_full, 1)

            pooled = [(xn_hi[:, 4 + b, :], xn_lo[:, 4 + b, :], Piece(10 + b).slot) for b in range(4)]
            scores(0)
            scores(1)
            pe.wait_ge(lo_done, 14)
            for j in range(NJ):
                n, kv = j // 2, j % 2
                if j + 2 < NJ:
                    scores(j + 2)
                pe.wait_ge(p_normed, j + 1)
                if j:
                    pe.wait_ge(pT_ready, j)
                pT = ps[:, 4:6, :].rearrange("p a (h q) -> p a h q", q=P)
                for kt in range(2):
                    for h in range(QH):
                        ins = pe.transpose(pT[:, kt, h, :], prob[j % 3][:, h, kt * P:(kt + 1) * P], ident[:, :])
                ins.then_inc(t_full, 1)
                if j:
                    pe.wait_ge(po_added, j)
                rows(ps[:, 7, :], j, pooled).then_inc(po_full, 1)
                pe.wait_ge(pT_ready, j + 1)
                if j:
                    pe.wait_ge(cat_done, j)
                for kt in range(2):
                    ins = pe.matmul(ps[64 * kv:64 * kv + 64, 6, :], vt[:, n + kt, 64 * kv:64 * kv + 64],
                                    probT[:, kt, :, :].rearrange("p h q -> p (h q)"), start=kt == 0, stop=kt == 1)
                ins.then_inc(v_full, 1)

            pe.wait_ge(lo_done, NA)
            pe.wait_ge(cat_done, NJ)
            pe.wait_ge(po_added, NJ)
            outputs([(xn_hi[:, b, :], xn_lo[:, b, :], Piece(14 + b).slot) for b in range(4)], with_norm=True)

            def gate_up(n0, i, turns):
                for b in range(FB):
                    gu = [Piece(n0 + 2 * b + m, i, RP, turns) for m in range(2)]
                    pe.wait_ge(lo_done, gu[1].count(1))
                    for half in range(2):
                        p = begin_unit()
                        columns(p[:, 0, :], gu[0], half)
                        columns(p[:, 1, :], gu[1], half).then_inc(pair_full, 1)
                        t.add("gu")

            def down(n0, i, turns, with_norm=False):
                pe.wait_ge(lo_done, Piece(n0 + 5, i, RP, turns).count(1))

                def hidden_split(n):
                    if n % NT == 0:
                        pe.wait_ge(h_split, t.count("gu", n // NT - 1))
                outputs([(h_hi[:, b, :], h_lo[:, b, :], 4 + b) for b in range(FB)], with_norm, hidden_split)

            def ffn(layer, with_norm):
                n0 = FFN_AT[layer]
                gate_up(n0, None, 1)
                with pe.Fori(0, ROUNDS - 1) as i:
                    t.enter(i, unit=2 * FB, gu=2 * FB, out=2 * NT)
                    down(n0, i, ROUNDS - 1)
                    gate_up(n0 + RP, i, ROUNDS - 1)
                    t.leave(ROUNDS - 1)
                down(n0 + RP * (ROUNDS - 1), None, 1, with_norm)

            pe.wait_ge(pair_freed, t.count("unit"))
            ffn(0, True)

            pe.wait_ge(pair_freed, t.count("unit"))
            pe.wait_ge(wdt_split, 1)
            p = begin_unit()
            for tt in range(NT):
                tok = slice(tt * P, (tt + 1) * P)
                for k in range(NK):
                    ins = mm3(p[:, 0, tt * SH:(tt + 1) * SH], xn_hi[:, k, tok], xn_lo[:, k, tok],
                              wdt_hi[:, k, :], wdt_lo[:, k, :], k == 0, k == NK - 1)
            ins.then_inc(pair_full, 1)
            pe.wait_ge(dts_v, 4)
            p = begin_unit()
            for m, w in enumerate((tri, ones)):
                for n, d in enumerate((gda_hi, gda_lo)):
                    ins = pe.matmul(p[:, m, 0:G * NT * HG], w[:, :], d[:, :, :].rearrange("p g k -> p (g k)"),
                                    start=n == 0, stop=n == 1)
            ins.then_inc(pair_full, 1)

            with pe.Fori(0, G) as g:
                t.enter(g, unit=NCB + BG, conv=NCB, z=BG, chunk=NT, half=2 * NT, out=2 * NT)
                for k in range(NCB):
                    project(Piece(SSD0 + k, g, GP, G))
                    t.add("conv")

                def token_major(c):
                    tok = slice(c * P, (c + 1) * P)
                    if c:
                        pe.wait_ge(cb_freed, t.count("chunk", c))
                    pe.matmul(ps[:, 2, 0:P], BT[:, tok], CT[:, tok], start=True, stop=True)
                    pe.transpose(ps[:, 2, P:2 * P], BT[:, tok], ident[:, :]).then_inc(cb_full, 1)
                    if c:
                        pe.wait_ge(xdt_ready, t.count("chunk", c))
                    for b in range(BG):
                        ins = pe.transpose(ps[:, 3, b * P:(b + 1) * P], yx[:, b, tok], ident[:, :])
                    ins.then_inc(xsT_full, 1)

                def decay_sums(c):
                    for hf in range(2):
                        k = 2 * c + hf
                        if k >= 3:
                            pe.wait_ge(m_ready, t.count("half", k - 2))
                        for h in range(4):
                            for n, d in enumerate((da_hi, da_lo)):
                                col = c * HG + 4 * hf + h
                                ins = pe.matmul(ps[:, BC_BANKS[k % 3], h * P:(h + 1) * P],
                                                d[:, col:col + 1].to_broadcast([P, P]), tri[:, :], start=n == 0, stop=n == 1)
                        ins.then_inc(bc_full, 1)

                pe.wait_ge(silu_done, t.count("conv"))
                pe.wait_ge(out_added, t.count("out"))
                token_major(0)
                decay_sums(0)
                for c in range(NT):
                    tok = slice(c * P, (c + 1) * P)
                    if c + 1 < NT:
                        token_major(c + 1)
                    pe.wait_ge(xds_ready, t.count("chunk", c + 1))
                    if c:
                        pe.wait_ge(state_ready, t.count("chunk", c))
                    pe.matmul(ps[:, 7, :], btok[:, :], xds[:, :], start=True, stop=True).then_inc(states_full, 1)
                    if c:
                        pe.wait_ge(yoff_read, t.count("chunk", c))
                        for b in range(BG):
                            ins = pe.matmul(ps[:, 5, b * P:(b + 1) * P], state[:, b * P:(b + 1) * P], CT[:, tok],
                                            start=True, stop=True)
                        ins.then_inc(yoff_full, 1)
                    if c + 1 < NT:
                        decay_sums(c + 1)
                    pe.wait_ge(m_ready, t.count("half", 2 * c + 2))
                    if c:
                        pe.wait_ge(y_ready, t.count("chunk", c))
                    for h in range(HG):
                        ins = pe.matmul(ps[64 * (h % 2):64 * (h % 2) + 64, 4, (h // 2) * P:(h // 2 + 1) * P],
                                        xdt[c % 2][:, h * PH:(h + 1) * PH], mdec[:, h, :], start=True, stop=True)
                    ins.then_inc(ydiag_full, 1)
                t.add("chunk", NT)
                t.add("half", 2 * NT)

                def square_sums():
                    pe.wait_ge(sq_ready, t.count("z", 1))
                    k = t.n["z"] % BG
                    for tt in range(NT):
                        ins = pe.matmul(ps[:, 4, k * NT + tt:k * NT + tt + 1], sq[:, tt * P:(tt + 1) * P], one_col,
                                        start=True, stop=True)
                    ins.then_inc(ssq_full, 1)
                    t.add("z")

                pe.wait_ge(y_ready, t.count("chunk"))
                for k in range(BG):
                    project(Piece(SSD0 + NCB + k, g, GP, G))
                    if k:
                        square_sums()
                square_sums()
                pe.wait_ge(lo_done, Piece(SSD0 + GP - 1, g, GP, G).count(1))
                pe.wait_ge(y_split, t.count("z"))
                pe.wait_ge(ssq_sum, g + 1)
                outputs([(y_hi[:, b, :], y_lo[:, b, :], ssd_slots[NCB + BG + b]) for b in range(BG)])
                t.leave(G)

            for tt in range(NT):
                norm_T(tt)
            pe.wait_ge(pair_freed, t.count("unit"))
            ffn(1, False)

        @block.vector
        def _(dve):
            t = Tally(unit=0, out=0, tile=0, conv=0, z=0, gu=0, chunk=0, half=0, step=0)

            def step(ins):
                ins.then_inc(step_done, 1)
                t.add("step")
                dve.wait_ge(step_done, t.count("step"))

            def unit(full=True):
                if full:
                    dve.wait_ge(pair_full, t.count("unit", 1))
                return flat(pair(t.n["unit"]))

            def freed(ins):
                ins.then_inc(pair_freed, 1)
                t.add("unit")

            def add_out(scale=None):
                n = t.n["out"] % (2 * NT)
                tt, half = n // 2, n % 2
                bank = ps[:, 4 + n % 4, :]
                dve.wait_ge(out_full, t.count("out", 1))
                if t.i is not None or t.n["out"] >= 2 * NT:
                    dve.wait_ge(out_added, t.count("out", 1 - 2 * NT))
                dst = xres[:, tt, half * BANK:(half + 1) * BANK]
                if scale is None:
                    ins = dve.tensor_tensor(dst, bank, dst, ALU.add)
                else:
                    ins = dve.scalar_tensor_tensor(dst, bank, scale[:, tt:tt + 1], dst, ALU.mult, ALU.add)
                ins.then_inc(out_added, 1)
                t.add("out")

            def normed(n_norm, tt, dst):
                dve.wait_ge(std_ready, NT * n_norm + tt + 1)
                dve.reciprocal(rstd[:, tt:tt + 1], std[:, tt:tt + 1]).then_inc(rstd_ready, 1)
                dve.wait_ge(rstd_ready, NT * n_norm + tt + 1)
                if tt == 0:
                    dve.wait_ge(norm_w_loaded, 16 * (n_norm + 1))
                return dve.scalar_tensor_tensor(dst[:, :], xres[:, tt, :], rstd[:, tt:tt + 1], norm_w[:, :],
                                                ALU.mult, ALU.mult)

            def norm(n_norm, with_outs):
                unit0 = t.n["unit"]

                def make(tt):
                    if tt >= 2:
                        dve.wait_ge(pair_full, unit0 + tt - 1)
                    normed(n_norm, tt, xn[tt % 2]).then_inc(xn_ready, 1)

                def lo(tt):
                    dve.wait_ge(xn_hi_done, NT * n_norm + tt + 1)
                    tok = slice(tt * P, (tt + 1) * P)
                    freed(dve.tensor_tensor(xn_lo[:, :, tok], pair(unit0 + tt).rearrange("p a (b c) -> p (a b) c", c=P),
                                            f(xn_hi[:, :, tok]), ALU.subtract))
                for tt in range(NT):
                    if with_outs:
                        add_out()
                        add_out()
                    if tt >= 1:
                        make(tt - 1)
                    if tt >= 3:
                        lo(tt - 3)
                make(NT - 1)
                for tt in range(NT - 3, NT):
                    lo(tt)

            dve.wait_ge(masks_ready, 13 + PAD)
            norm(0, False)
            dve.wait_ge(const_T, 1)
            NB = CC // P
            c0, c1 = ps[:, 4, 0:(CONV + 1) * NB], ps[:, 4, P:P + G * BG + 4]
            for tap in range(CONV + 1):
                for k in range(2):
                    j = tap * NB + INNER // P + k * G
                    col = GC_TAP + k * CONV + tap if tap < CONV else GC_BIAS + k
                    dve.tensor_copy(gconst[:, :, col], c0[:, j:j + G])
                for b in range(BG):
                    col = GC_TAP + (2 + b) * CONV + tap if tap < CONV else GC_BIAS + 2 + b
                    dve.tensor_copy(gconst[:, :, col], c0[:, tap * NB + b:tap * NB + G * BG:BG])
            dve.tensor_copy(gconst[:, :, GC_NW:GC_NW + BG], c1[:, 0:G * BG].rearrange("p (g b) -> p g b", b=BG))
            for odd in range(2):
                hd = slice(64 * odd, 64 * odd + 64)
                dve.tensor_copy(gconst[hd, :, GC_D:GC_D + BG],
                                rep[hd, odd::2].rearrange("p (g b) -> p g b", b=BG))
            dve.tensor_scalar(neg_sink[:, :], sink, -1.0, None, ALU.mult)
            dve.tensor_copy(p_scale, c1[:, G * BG:G * BG + 4]).then_inc(const_ready, 1)

            for b in range(4):
                w = WINDOWS[b]
                dve.memset(u[b][:, 0:PAD], 0.0)
                if b == 0:
                    for i in range(2):
                        dve.memset(win[i][:, 0:PAD], 0.0)
                freed(dve.tensor_copy(u[b][:, PAD:], unit()))
                dve.wait_ge(pair_freed, t.count("unit"))
                src, shift, n = u[b], 1, 0
                while shift < w:
                    dst = win[n % 2]
                    step(dve.tensor_tensor(dst[:, PAD:], src[:, PAD:], src[:, PAD - shift:PAD + S - shift], ALU.add))
                    src, shift, n = dst, 2 * shift, n + 1
                step(dve.tensor_tensor(src[:, PAD:PAD + w], src[:, PAD:PAD + w], inv_count[:, 0:w], ALU.mult))
                dve.tensor_tensor(u[b][:, PAD:PAD + w], src[:, PAD:PAD + w], u[b][:, PAD:PAD + w], ALU.subtract)
                dve.scalar_tensor_tensor(u[b][:, PAD + w:], src[:, PAD + w:], 1.0 / w, u[b][:, PAD + w:],
                                         ALU.mult, ALU.subtract).then_inc(d_ready, 1)
            for i in range(4):
                freed(dve.tensor_copy(qT[:, i, :], unit()))
            dve.memset(kT[:, 0:P], 0.0)
            freed(dve.tensor_copy(kT[:, P:], unit()))
            dve.memset(vt[:, 0, :], 0.0)
            freed(dve.tensor_copy(vt[:, 1:, :].rearrange("p a b -> p (a b)"), unit()))
            for b in range(4):
                dve.wait_ge(cat_hi_done, b + 1)
                freed(dve.scalar_tensor_tensor(xn_lo[:, 4 + b, :], unit(), p_scale[:, b:b + 1],
                                               f(xn_hi[:, 4 + b, :]), ALU.mult, ALU.subtract))

            NJ = 2 * NT

            def scores(j):
                n, kv, r = j // 2, j % 2, j % 3
                if j >= 3:
                    dve.wait_ge(t_full, j - 2)
                hd = slice(kv * QH, (kv + 1) * QH)
                m = masks[:, min(n, 1), :].unsqueeze(1).to_broadcast([P, QH, 2 * P])
                unit()
                freed(dve.scalar_tensor_tensor(prob[r][:, :, :],
                                               pair(t.n["unit"]).rearrange("p a (b c) -> p (a b) c", c=2 * P),
                                               float(HEAD_DIM) ** -0.5, m, ALU.mult, ALU.add))
                dve.wait_ge(pair_freed, t.count("unit"))
                step(dve.reduce_max(row_max[r], prob[r][:, :, :], AX_X))
                step(dve.scalar_tensor_tensor(neg_max[r], row_max[r], -1.0, neg_sink[:, hd], ALU.mult, ALU.min))
                dve.tensor_tensor(sink_exp[r], neg_max[r], sink[:, hd], ALU.add).then_inc(max_ready, 1)

            def row_sums(j):
                r = j % 3
                dve.wait_ge(p_ready, j + 1)
                step(dve.tensor_tensor(row_sum[r], row_sum[r], sink_exp[r], ALU.add))
                dve.reciprocal(row_sum[r], row_sum[r]).then_inc(rsum_ready, 1)

            def v_lo(j):
                hd = slice(64 * (j % 2), 64 * (j % 2) + 64)
                tok = slice((j // 2) * P, (j // 2 + 1) * P)
                dve.wait_ge(cat_hi_done, 4 + j + 1)
                dve.tensor_tensor(xn_lo[hd, 0:QH, tok], ps[hd, 6, :].rearrange("p (h q) -> p h q", q=P),
                                  f(xn_hi[hd, 0:QH, tok]), ALU.subtract).then_inc(cat_done, 1)

            scores(0)
            scores(1)
            row_sums(0)
            for j in range(NJ):
                if j + 2 < NJ:
                    scores(j + 2)
                if j + 1 < NJ:
                    row_sums(j + 1)
                if j >= 1:
                    v_lo(j - 1)
                dst = xres[:, j // 2, j % 2 * BANK:(j % 2 + 1) * BANK]
                dve.wait_ge(po_full, j + 1)
                dve.tensor_tensor(dst, ps[:, 7, :], dst, ALU.add).then_inc(po_added, 1)
            v_lo(NJ - 1)
            dve.wait_ge(po_added, NJ)
            norm(1, True)

            def gate_up():
                for k in range(2 * FB):
                    dve.wait_ge(pair_full, t.count("unit", 1))
                    dve.wait_ge(gate_done, t.count("gu", 1))
                    freed(dve.tensor_tensor(hid[k % 2][:, :], pair(t.n["unit"])[:, 1, :], gate[k % 2][:, :], ALU.mult))
                    t.add("gu")
                    dve.wait_ge(h_hi_done, t.count("gu"))
                    tok = slice((k % 2) * BANK, (k % 2 + 1) * BANK)
                    dve.tensor_tensor(h_lo[:, k // 2, tok], hid[k % 2][:, :], f(h_hi[:, k // 2, tok]), ALU.subtract)\
                        .then_inc(h_split, 1)

            def ffn():
                gate_up()
                with dve.Fori(0, ROUNDS - 1) as i:
                    t.enter(i, unit=2 * FB, gu=2 * FB, out=2 * NT)
                    for _ in range(2 * NT):
                        add_out()
                    gate_up()
                    t.leave(ROUNDS - 1)

            ffn()
            norm(2, True)

            dtv, w1, eq, dA, dm, lu = D[0], D[3], D[5], D[6], D[6], D[7]

            def tiles(row):
                return row.unsqueeze(1).to_broadcast([P, NT, SH])

            freed(dve.tensor_tensor(dtv[:, :, :], unit()[:, 0:NT * SH].rearrange("p (c s) -> p c s", s=SH),
                                    tiles(dt_bias), ALU.add))
            dve.wait_ge(pair_freed, t.count("unit"))
            dve.scalar_tensor_tensor(D[1][:, :, :], dtv[:, :, :], -1.0, dtv[:, :, :], ALU.mult, ALU.max).then_inc(dts_v, 1)
            dve.wait_ge(dts_a, 1)
            dve.tensor_scalar(w1[:, :, :], D[2][:, :, :], 1.0, None, ALU.add).then_inc(dts_v, 1)
            dve.wait_ge(dts_v, 2)
            dve.scalar_tensor_tensor(eq[:, :, :], w1[:, :, :], 1.0, D[2][:, :, :], ALU.is_equal, ALU.mult)
            step(dve.tensor_scalar(dm[:, :, :], w1[:, :, :], 1.0, 1e-30, ALU.subtract, ALU.max))
            dve.reciprocal(dm[:, :, :], dm[:, :, :])
            dve.wait_ge(dts_a, 3)
            step(dve.tensor_tensor(lu[:, :, :], D[4][:, :, :], D[2][:, :, :], ALU.mult))
            step(dve.tensor_tensor(lu[:, :, :], lu[:, :, :], dm[:, :, :], ALU.mult))
            step(dve.tensor_tensor(lu[:, :, :], lu[:, :, :], eq[:, :, :], ALU.add))
            step(dve.scalar_tensor_tensor(dtv[:, :, :], dtv[:, :, :], 0.0, lu[:, :, :], ALU.max, ALU.add))
            dve.scalar_tensor_tensor(dA[:, :, :], dtv[:, :, :], -1.0, tiles(exp_a), ALU.mult, ALU.mult).then_inc(dts_v, 1)

            def by_group(d):
                return d[:, :, :].rearrange("p c (g h) -> p g c h", h=HG)

            def group_major(ap):
                return ap.rearrange("p g (c h) -> p g c h", h=HG)

            dve.tensor_copy(group_major(gconst[:, :, GC_DT:GC_DT + NT * HG]), by_group(dtv))
            dve.wait_ge(dts_a, 4)
            dve.tensor_tensor(group_major(gda_lo[:, :, :]), by_group(dA), group_major(f(gda_hi[:, :, :])), ALU.subtract)\
                .then_inc(dts_v, 1)
            sums = unit()
            acs = gconst[:, :, GC_ACS:GC_ACS + NT * HG]

            def flat_g(ap):
                return ap.rearrange("p (g k) -> p g k", g=G)
            dve.tensor_copy(acs, flat_g(sums[:, 0:G * NT * HG]))
            freed(dve.tensor_copy(D[7][:, :, :].rearrange("p c s -> p (c s)"), sums[:, BANK:BANK + G * NT * HG]))
            dve.wait_ge(pair_freed, t.count("unit"))
            dve.tensor_tensor(flat_g(D[3][:, :, :].rearrange("p c s -> p (c s)")),
                              flat_g(D[7][:, :, :].rearrange("p c s -> p (c s)")), acs, ALU.subtract).then_inc(dts_v, 1)
            dve.wait_ge(dts_a, 6)

            with dve.Fori(0, G) as g:
                t.enter(g, unit=NCB + BG, conv=NCB, z=BG, chunk=NT, half=2 * NT, out=2 * NT, step=(CONV - 2) * NCB + NT - 1)

                def group(ap):
                    return ap[:, bass.ds(g, 1), :].rearrange("p g k -> p (g k)")
                dve.tensor_copy(gc[:, :], group(gconst))
                dve.tensor_copy(da_hi[:, :], group(f(gda_hi[:, :, :])))
                dve.tensor_copy(da_lo[:, :], group(f(gda_lo[:, :, :]))).then_inc(gc_ready, 1)
                dve.wait_ge(gc_ready, g + 1)
                for k in range(NCB):
                    full = unit()
                    dve.wait_ge(acc_ready, t.count("conv", 1))
                    for shift in range(1, CONV):
                        tap = GC_TAP + k * CONV + CONV - 1 - shift
                        ins = dve.scalar_tensor_tensor(acc[k % 2][:, shift:], full[:, 0:S - shift], gc[:, tap:tap + 1],
                                                       acc[k % 2][:, shift:], ALU.mult, ALU.add)
                        if shift < CONV - 1:
                            step(ins)
                        else:
                            freed(ins)
                    t.add("conv")

                def token_major(c):
                    dve.wait_ge(cb_full, t.count("chunk", c + 1))
                    if c == 0:
                        dve.wait_ge(silu_done, t.count("conv"))
                    dve.tensor_tensor(cbm[c % 2][:, :], ps[:, 2, 0:P], f(tri[:, :]), ALU.mult)
                    if c:
                        dve.wait_ge(states_full, t.count("chunk", c))
                    dve.tensor_copy(btok[:, :], ps[:, 2, P:2 * P]).then_inc(cb_freed, 1)
                    dve.wait_ge(xsT_full, t.count("chunk", c + 1))
                    if c >= 2:
                        dve.wait_ge(ydiag_full, t.count("chunk", c - 1))
                    dve.tensor_tensor(xdt[c % 2][:, :].rearrange("p (h d) -> p h d", d=PH),
                                      ps[:, 3, :].rearrange("p (h d) -> p h d", d=PH),
                                      gc[:, GC_DT + c * HG:GC_DT + (c + 1) * HG].unsqueeze(2).to_broadcast([P, HG, PH]),
                                      ALU.mult).then_inc(xdt_ready, 1)

                token_major(0)
                for c in range(NT):
                    tok = slice(c * P, (c + 1) * P)
                    if c:
                        dve.wait_ge(ydiag_full, t.count("chunk", c))
                    for hf in range(2):
                        dve.wait_ge(dec_ready, t.count("half", 2 * c + hf + 1))
                        if hf == 0:
                            dve.wait_ge(cb_freed, t.count("chunk", c + 1))
                        dve.tensor_tensor(mdec[:, 4 * hf:4 * hf + 4, :],
                                          ps[:, BC_BANKS[(2 * c + hf) % 3], :].rearrange("p (h l) -> p h l", l=P),
                                          cbm[c % 2][:, :].unsqueeze(1).to_broadcast([P, 4, P]), ALU.mult)\
                            .then_inc(m_ready, 1)
                    if c + 1 < NT:
                        token_major(c + 1)
                    dve.wait_ge(states_full, t.count("chunk", c + 1))
                    if c:
                        dve.wait_ge(decayed_ready, g * (NT - 1) + c)
                        dve.wait_ge(yoff_full, g * (NT - 1) + c)
                        dve.tensor_tensor(state[:, :], ps[:, 7, :], decayed[:, :], ALU.add).then_inc(state_ready, 1)
                    else:
                        dve.tensor_copy(state[:, :], ps[:, 7, :]).then_inc(state_ready, 1)
                    dve.wait_ge(e_ready, t.count("half", 2 * c + 2))
                    e = eacs[c % 2]
                    e2 = e[:, :, :].rearrange("p b l -> p (b l)")
                    if c:
                        dve.tensor_tensor(e2, ps[:, 5, :], e2, ALU.mult).then_inc(yoff_read, 1)
                        dve.wait_ge(yoff_read, t.count("chunk", c + 1))
                        dve.wait_ge(ydiag_full, t.count("chunk", c + 1))
                        step(dve.tensor_tensor(e2, ps[:, 4, :], e2, ALU.add))
                    else:
                        dve.wait_ge(ydiag_full, t.count("chunk", c + 1))
                        dve.tensor_copy(e2, ps[:, 4, :]).then_inc(yoff_read, 1)
                        dve.wait_ge(yoff_read, t.count("chunk", c + 1))
                    for b in range(BG):
                        d = gc[:, GC_D + b:GC_D + b + 1]
                        ins = dve.scalar_tensor_tensor(yx[:, b, tok], yx[:, b, tok], d, e[:, b, :], ALU.mult, ALU.add)
                    ins.then_inc(y_ready, 1)
                t.add("chunk", NT)
                t.add("half", 2 * NT)
                dve.wait_ge(y_ready, t.count("chunk"))
                for k in range(BG):
                    pz = unit()
                    dve.wait_ge(z_done, t.count("z", 1))
                    freed(dve.tensor_tensor(yx[:, k, :], pz, yx[:, k, :], ALU.mult))
                    t.add("z")
                    dve.wait_ge(y_hi_done, t.count("z"))
                    dve.scalar_tensor_tensor(y_lo[:, k, :], yx[:, k, :], gc[:, GC_NW + k:GC_NW + k + 1],
                                             f(y_hi[:, k, :]), ALU.mult, ALU.subtract).then_inc(y_split, 1)
                dve.wait_ge(ssq_full, t.count("z"))
                dve.reduce_sum(rms, ps[:, 4, 0:BG * NT].rearrange("p (k t) -> p t k", t=NT), AX_X).then_inc(ssq_sum, 1)
                dve.wait_ge(rms_rooted, g + 1)
                dve.reciprocal(rms, rms).then_inc(rms_ready, 1)
                dve.wait_ge(rms_ready, g + 1)
                for _ in range(2 * NT):
                    add_out(rms)
                t.leave(G)

            dve.wait_ge(out_added, t.count("out"))
            norm(3, False)
            ffn()
            for tt in range(NT):
                add_out()
                add_out()
                if tt >= 1:
                    if tt >= 3:
                        dve.wait_ge(stored[(tt - 1) % 2], 16 * ((tt - 1) // 2))
                    normed(4, tt - 1, xn[(tt - 1) % 2]).then_inc(final_ready, 1)
            dve.wait_ge(stored[(NT - 1) % 2], 16 * ((NT - 1) // 2))
            normed(4, NT - 1, xn[(NT - 1) % 2]).then_inc(final_ready, 1)


INPUTS = ["x", "mix_norm_w", "ap_w_in", "ap_sinks", "pool_w", "pool_scale", "ap_w_out", "ssd_w_in", "ssd_conv_w",
          "ssd_conv_b", "ssd_dt_bias", "ssd_A_log", "ssd_D", "ssd_norm_w", "ssd_w_out", "ffn_norm_w", "w_gate",
          "w_up", "w_down", "final_norm_w"]


def kernel(**inputs):
    import numpy as np
    import concourse.bacc as bacc
    from concourse.bass_utils import run_bass_kernel_spmd

    nc = bacc.Bacc("TRN2", target_bir_lowering=False, num_devices=1)
    arrays, args = {}, []
    for name in INPUTS:
        a = np.ascontiguousarray(inputs[name])
        arrays[f"in_{name}"] = a
        args.append(nc.dram_tensor(f"in_{name}", a.shape, mybir.dt.from_np(a.dtype), kind="ExternalInput").ap())
    out = nc.dram_tensor("out", inputs["x"].shape, F32, kind="ExternalOutput").ap()
    trunk(nc, *args, out)
    r = run_bass_kernel_spmd(nc, [arrays], core_ids=[0])
    return r.results[0]["out"]
```

```python
from contextlib import ExitStack

import concourse.bass as bass
from concourse import mybir

F32 = mybir.dt.float32
F32R = mybir.dt.float32r
ALU = mybir.AluOpType
ACT = mybir.ActivationFunctionType
AX_X = mybir.AxisListType.X

P = 128
EPS = 1e-5
NEG = -1e30
WINDOWS = (2, 4, 8, 16)
KV_HEADS, HEADS, HEAD_DIM = 2, 8, 64
PAD = 16
RAW_SLOTS = 2
SPLIT_SLOTS = 6
LEAD = 4
BANK = 512


class Tally:

    def __init__(self, **starts):
        self.n = dict(starts)
        self.i, self.per, self.start = None, {}, {}

    def count(self, name, more=0):
        v = self.n[name] + more
        return v if self.i is None or not self.per.get(name) else self.i * self.per[name] + v

    def add(self, name, k=1):
        self.n[name] += k

    def enter(self, i, **per):
        self.i, self.per, self.start = i, per, dict(self.n)

    def leave(self, trips):
        for name, v in self.n.items():
            per = v - self.start[name]
            assert per == self.per.get(name, 0), (name, per)
            self.n[name] = self.start[name] + per * trips
        self.i = None


def trunk(nc, x, mix_norm_w, ap_w_in, ap_sinks, pool_w, pool_scale, ap_w_out, ssd_w_in, ssd_conv_w,
          ssd_conv_b, ssd_dt_bias, ssd_A_log, ssd_D, ssd_norm_w, ssd_w_out, ffn_norm_w, w_gate, w_up,
          w_down, final_norm_w, out):
    S, DM = x.shape[1], x.shape[2]
    NT = S // P
    NK = DM // P
    AW = HEADS * HEAD_DIM
    QH = HEADS // KV_HEADS
    FF = w_gate.shape[2]
    NF = FF // P
    FB = 2
    ROUNDS = NF // FB
    INNER = ssd_w_out.shape[1]
    SH = ssd_D.shape[1]
    PH = INNER // SH
    G = 4
    HG = SH // G
    BG = INNER // P // G
    CONV = ssd_conv_w.shape[1]
    CC = ssd_conv_w.shape[2]
    NCB = BG + 2
    assert S == NT * P == 1024 and DM == 1024 and NF == FB * ROUNDS and HG == 8 and BG == 4
    assert CONV == 4 and P == 128 and ap_w_in.shape[2] == AW + 2 * P + 4 * P

    GC_TAP, GC_BIAS = 0, NCB * CONV
    GC_D, GC_NW = GC_BIAS + NCB, GC_BIAS + NCB + BG
    GC_DT = GC_NW + BG
    GC_ACS, GC_DS, GC_CD = GC_DT + NT * HG, GC_DT + 2 * NT * HG, GC_DT + 3 * NT * HG
    GC = GC_DT + 4 * NT * HG

    ap_in = ap_w_in[0]
    pool_cols = [ap_in[:, AW + 2 * P + b * P:AW + 2 * P + (b + 1) * P].rearrange("(k p) c -> p k c", p=P)
                 for b in range(4)]
    kv_cols = [ap_in[:, AW + b * P:AW + (b + 1) * P].rearrange("(k p) c -> p k c", p=P) for b in range(2)]
    zc, xc = 0, INNER // P
    bc_, cc_ = xc + INNER // P, xc + INNER // P + G
    dtc = 2 * INNER + 2 * G * P

    with ExitStack() as ctx:
        def sb(name, shape, dt=F32):
            return ctx.enter_context(nc.sbuf_tensor(name, shape, dt))

        def sem(name):
            return ctx.enter_context(nc.semaphore(name))

        xres = sb("xres", [P, NT, DM])
        xn_hi = sb("xn_hi", [P, NK, S], F32R)
        xn_lo = sb("xn_lo", [P, NK, S], F32R)
        raw = [sb(f"w_raw{i}", [P, DM]) for i in range(RAW_SLOTS)]
        w_hi = [sb(f"w_hi{i}", [P, DM], F32R) for i in range(SPLIT_SLOTS)]
        w_lo = [sb(f"w_lo{i}", [P, DM], F32R) for i in range(SPLIT_SLOTS - 1)]
        slot5_at = [nc.sbuf_base - SPLIT_SLOTS * 4 * DM, nc.sbuf_base]
        w_lo.append(sb("w_lo5", [P, DM], F32R))
        ident = sb("ident", [P, P])
        tri = sb("tri", [P, P], F32R)
        ones = sb("ones", [P, P], F32R)
        gconst = sb("gconst", [P, G, GC])
        gda_at = nc.sbuf_base
        gda_hi = sb("gda_hi", [P, G, NT * HG], F32R)
        gda_lo = sb("gda_lo", [P, G, NT * HG], F32R)
        gc = sb("gc", [P, GC])
        da_hi = sb("da_hi", [P, NT * HG], F32R)
        da_lo = sb("da_lo", [P, NT * HG], F32R)
        small = sb("small", [P, 176])
        eps = sb("eps", [P, 1])
        sink, dt_bias, exp_a, p_scale = small[:, 0:8], small[:, 8:40], small[:, 40:72], small[:, 72:76]
        ssq, std, rstd = small[:, 76:84], small[:, 84:92], small[:, 92:100]
        row_max, neg_max, row_sum, sink_exp = (
            [small[:, a + 4 * r:a + 4 * r + 4] for r in range(3)] for a in (100, 112, 124, 136))
        rms = small[:, 148:156]
        inv_count, one_col, neg_sink = small[:, 156:172], small[:, 172:173], sb("neg_sink", [P, 8])

        shared_at = nc.sbuf_base
        assert shared_at % 32 == 0 and gda_at % 32 == 0
        SHARED = 7 * S + 4 * S + P
        sb("shared", [P, SHARED])

        def at(name, start, shape, dt=F32, origin=shared_at):
            n = 1
            for d in shape:
                n *= d
            assert origin != shared_at or start + n <= SHARED
            return nc.alloc_sbuf_tensor_at(name, [P] + shape, dt, offset=origin + 4 * start)

        norm_w = at("norm_w", 0, [DM])
        masks = at("masks", 0, [2, 2 * P], origin=gda_at)
        stage = at("stage", 3072, [2, P])
        rep = at("rep", 3072 + 2 * P, [SH])
        qT = at("qT", 0, [4, S])
        kT = at("kT", 4 * S, [S + P])
        v_ch = at("v_ch", 3 * S, [S])
        vt = at("vt", 4 * S + (S + P), [NT + 1, P])
        UO = 4 * S + 2 * (NT + 1) * P
        u = [at(f"u{b}", UO + b * (PAD + S), [PAD + S]) for b in range(4)]
        win = [at(f"win{i}", 4 * S + i * (S + P), [PAD + S]) for i in range(2)]
        pool_wt = at("pool_wt", UO + 4 * (PAD + S), [4, P])
        prob = [at(f"prob{r}", UO + r * 1024, [QH, 2 * P]) for r in range(3)]
        probT = at("probT", UO + 3 * 1024, [2, QH, P])
        h_hi = at("h_hi", 1024, [FB, S], F32R)
        h_lo = at("h_lo", 3072, [FB, S], F32R)
        gate = [at(f"gate{i}", 5120 + i * BANK, [BANK]) for i in range(2)]
        hid = [at(f"hid{i}", 6144 + i * BANK, [BANK]) for i in range(2)]
        xn = [at(f"xn{i}", 7168 + i * DM, [DM]) for i in range(2)]
        junk = at("junk", 9216, [DM])
        wdt = at("wdt", 10240, [NK, SH])
        wdt_hi = at("wdt_hi", 10496, [NK, SH], F32R)
        wdt_lo = at("wdt_lo", 10752, [NK, SH], F32R)
        dtT = at("dtT", 2048 + 256, [S])
        D = [at(f"dtmp{i}", 2048 + i * 256, [NT, SH]) for i in range(8)]
        BT, CT = at("BT", 0, [S]), at("CT", 1024, [S])
        acc = [at(f"acc{i}", 2048 + i * 1024, [S]) for i in range(2)]
        mdec = at("mdec", 2048, [HG, P])
        xdt = [at(f"xdt{i}", 3072 + i * BANK, [HG * PH]) for i in range(2)]
        xds = at("xds", 4096, [HG * PH])
        btok = at("btok", 4608, [P])
        cbm = [at(f"cbm{i}", 4736 + i * P, [P]) for i in range(2)]
        eacs = [at(f"eacs{i}", 4992 + i * BANK, [BG, P]) for i in range(2)]
        state, decayed = at("state", 6016, [HG * PH]), at("decayed", 6528, [HG * PH])
        y_hi = at("y_hi", 0, [BG, S], F32R)
        sq = [[at(f"sq{h}{b}", b * S + BANK if h == 0 else 4 * S + b * BANK, [BANK]) for b in range(BG)]
              for h in range(2)]
        zs = [at(f"zs{b}", b % 2 * BANK, [BANK], origin=slot5_at[b // 2]) for b in range(BG)]
        norm_w3, junk3 = at("norm_w3", 0, [DM], origin=slot5_at[0]), at("junk3", 0, [DM], origin=slot5_at[1])
        xn3 = [at(f"xn3{i}", 5 * S + i * DM, [DM]) for i in range(2)]
        yx = at("yx", 7 * S, [BG, S])
        y_lo = at("y_lo", 7 * S, [BG, S], F32R)

        ps = ctx.enter_context(nc.psum_tensor("ps", [P, 8, BANK], F32))

        def tail_pair(tt):
            return ps[:, 4 + 2 * (tt % 2):6 + 2 * (tt % 2), :]

        CB, XS, DECAY = 2, 3, 0
        YDIAG, YOFF, Z_BANK, STATES = 4, 5, 6, 7
        HI_AFTER_CHUNK = {0: 9, 1: 10, 4: 11, 5: 12, 6: 13}
        LO_AFTER_CHUNK = {1: 9, 2: 10, 5: 11, 6: 12, 7: 13}
        SSQ_AFTER_OUT = (0, 3)

        def pair(n):
            return ps[:, 2 * (n % 2):2 * (n % 2) + 2, :]

        def flat(ap):
            return ap.rearrange("p a b -> p (a b)")

        def f(ap):
            return ap.bitcast(F32)

        NA = 18
        RP, GP = 3 * FB, NCB + 2 * BG
        ssd_slots = [0, 1, 2, 3, 4, 0, 1, 2, 3, 0, 4, 1, 2, 3]
        seq = [(n % SPLIT_SLOTS, n % RAW_SLOTS) for n in range(NA)]
        for layer in range(2):
            FFN0 = len(seq)
            seq += [(n % SPLIT_SLOTS, n % RAW_SLOTS) for _ in range(ROUNDS) for n in range(RP)]
            if layer == 0:
                SSD0 = len(seq)
                seq += [(s, n % RAW_SLOTS) for _ in range(G) for n, s in enumerate(ssd_slots)]
        FFN_AT = (NA, FFN0)
        halves = set(range(6, 10)) | set(range(14, 18))

        class Piece:

            def __init__(self, n, i=None, per=0, turns=1):
                self.n, self.i, self.per = n, i, per
                all_ = [n + t * per for t in range(turns)]
                self.slot, self.raw = seq[n]
                assert all(seq[m] == seq[n] for m in all_)

                def back(m, which):
                    return next((d for d in range(1, m + 1) if seq[m - d][which] == seq[m][which]), None)

                def least(which):
                    got = [back(m, which) for m in all_]
                    return None if got[0] is None else min(got)
                self.slot_back, self.raw_back = least(0), least(1)

                def parts(m):
                    return sum(2 if k in halves else 1 for k in range(m + 1) if seq[k][1] == self.raw)
                self.parts = parts(n)
                self.parts_per = parts(n + per) - parts(n) if turns > 1 else 0

            def count(self, more=0):
                return self.n + more if self.i is None else self.i * self.per + (self.n + more)

            def raw_count(self):
                return 16 * self.parts if self.i is None else self.i * (16 * self.parts_per) + 16 * self.parts

        raw_ready = [sem(f"raw_ready{i}") for i in range(RAW_SLOTS)]
        hi_done, lo_done = sem("hi_done"), sem("lo_done")
        pair_full = sem("pair_full")
        pair_freed = sem("pair_freed")
        out_full = sem("out_full")
        out_added = sem("out_added")
        x_loaded = [sem(f"x_loaded{t}") for t in range(NT)]
        norm_w_loaded, const_loaded, wdt_loaded = sem("norm_w_loaded"), sem("const_loaded"), sem("wdt_loaded")
        masks_ready = sem("masks_ready")
        const_T, const_ready = sem("const_T"), sem("const_ready")
        ssq_ready, std_ready = sem("ssq_ready"), sem("std_ready")
        rstd_ready, xn_ready = sem("rstd_ready"), sem("xn_ready")
        xn_hi_done = sem("xn_hi_done")
        step_done = sem("step_done")
        d_ready = sem("d_ready")
        cat_hi_done, cat_done = sem("cat_hi_done"), sem("cat_done")
        max_ready, p_ready = sem("max_ready"), sem("p_ready")
        rsum_ready, p_normed = sem("rsum_ready"), sem("p_normed")
        tail_full, tail_split = sem("tail_full"), sem("tail_split")
        t_full, pT_ready = sem("t_full"), sem("pT_ready")
        v_full, po_full, po_added = sem("v_full"), sem("po_full"), sem("po_added")
        gate_done = sem("gate_done")
        h_hi_done, h_split = sem("h_hi_done"), sem("h_split")
        wdt_hi_done, wdt_split = sem("wdt_hi_done"), sem("wdt_split")
        dts_v, dts_a = sem("dts_v"), sem("dts_a")
        gc_ready = sem("gc_ready")
        acc_ready, silu_done = sem("acc_ready"), sem("silu_done")
        cb_full, xsT_full, bc_full = sem("cb_full"), sem("xsT_full"), sem("bc_full")
        cb_freed, xdt_ready, m_ready = sem("cb_freed"), sem("xdt_ready"), sem("m_ready")
        relu_done, dec_ready, e_ready = sem("relu_done"), sem("dec_ready"), sem("e_ready")
        xds_ready, decayed_ready = sem("xds_ready"), sem("decayed_ready")
        state_ready = sem("state_ready")
        states_full, yoff_full, ydiag_full = sem("states_full"), sem("yoff_full"), sem("ydiag_full")
        yoff_read, y_ready = sem("yoff_read"), sem("y_ready")
        sums_full, z_full, z_gated = sem("sums_full"), sem("z_full"), sem("z_gated")
        sq_summed, dt_full = sem("sq_summed"), sem("dt_full")
        sq_added = sem("sq_added")
        z_done, sq_ready, y_hi_done = sem("z_done"), sem("sq_ready"), sem("y_hi_done")
        y_split = sem("y_split")
        ssq_full, rms_rooted, rms_ready = sem("ssq_full"), sem("rms_rooted"), sem("rms_ready")
        final_ready = sem("final_ready")
        stored = [sem("stored0"), sem("stored1")]

        def in_group(g):
            if isinstance(g, int):
                return lambda k: Piece(SSD0 + g * GP + k)
            return lambda k: Piece(SSD0 + k, g, GP, G - 1)

        block = ctx.enter_context(nc.Block())

        @block.sync
        def _(sp):
            def load(piece, *srcs):
                if piece.raw_back is not None:
                    sp.wait_ge(lo_done, piece.count(1 - piece.raw_back))
                dst = raw[piece.raw]
                if len(srcs) == 2 and srcs[0].shape[0] == P:
                    v = dst[:, :].rearrange("p (k c) -> p k c", c=P)
                    for h, s in enumerate(srcs):
                        sp.dma_start(v[:, :, h * HEAD_DIM:(h + 1) * HEAD_DIM], s).then_inc(raw_ready[piece.raw], 16)
                elif len(srcs) == 2:
                    for h, s in enumerate(srcs):
                        sp.dma_start(dst[h * HEAD_DIM:(h + 1) * HEAD_DIM, :], s).then_inc(raw_ready[piece.raw], 16)
                else:
                    s = srcs[0]
                    d = dst[:, :] if len(s.shape) == 2 else dst[:, :].rearrange("p (k c) -> p k c", c=P)
                    sp.dma_start(d, s).then_inc(raw_ready[piece.raw], 16)

            NB = CC // P

            def load_constants():
                for dst, src in ((stage[0:CONV * NB, 0, :], ssd_conv_w[0].rearrange("t (b p) -> (t b) p", p=P)),
                                 (stage[CONV * NB:(CONV + 1) * NB, 0, :], ssd_conv_b[0].rearrange("(b p) -> b p", p=P)),
                                 (stage[0:G * BG, 1, :], ssd_norm_w[0].rearrange("(b p) -> b p", p=P)),
                                 (stage[G * BG:G * BG + 4, 1, :], pool_scale[0].rearrange("(b p) -> b p", p=P)),
                                 (sink, ap_sinks.to_broadcast([P, HEADS])), (dt_bias, ssd_dt_bias.to_broadcast([P, SH])),
                                 (exp_a, ssd_A_log.to_broadcast([P, SH])), (rep[:, :], ssd_D.to_broadcast([P, SH])),
                                 (pool_wt[:, :, :], pool_w[0].rearrange("g c d -> c g d"))):
                    sp.dma_start(dst, src).then_inc(const_loaded, 16)

            def q_half(h):
                return ap_in[:, h * HEAD_DIM:(h + 1) * HEAD_DIM].rearrange("(k p) c -> p k c", p=P)
            srcs = [(c,) for c in pool_cols]
            srcs += [(c,) for c in kv_cols] + [(q_half(i), q_half(i + 4)) for i in range(4)]
            srcs += [(ap_w_out[0, AW + b * P:AW + (b + 1) * P, :],) for b in range(4)]
            srcs += [tuple(ap_w_out[0, h * HEAD_DIM:(h + 1) * HEAD_DIM, :] for h in (i, i + 4)) for i in range(4)]
            for n, s in enumerate(srcs):
                load(Piece(n), *s)
                if n == 1:
                    load_constants()

            def ffn(layer):
                wg, wu, wd = w_gate[layer], w_up[layer], w_down[layer]
                rows = wd.rearrange("(j p) n -> p j n", p=P)
                with sp.Fori(0, ROUNDS) as i:
                    for b in range(FB):
                        for m, w in enumerate((wg, wu)):
                            blk = w.rearrange("(k p) (j c) -> p k j c", p=P, c=P)[:, :, bass.ds(i * FB + b, 1), :]
                            load(Piece(FFN_AT[layer] + 2 * b + m, i, RP, ROUNDS), blk.rearrange("p k j c -> p k (j c)"))
                    for b in range(FB):
                        blk = rows[:, bass.ds(i * FB + b, 1), :]
                        load(Piece(FFN_AT[layer] + 4 + b, i, RP, ROUNDS), blk.rearrange("p j n -> p (j n)"))

            ffn(0)
            w_in = ssd_w_in[0]
            blocks = w_in[:, 0:(dtc // P) * P].rearrange("(k p) (j c) -> p k j c", p=P, c=P)
            rows = ssd_w_out[0].rearrange("(j p) n -> p j n", p=P)

            def ssd_group(g):
                piece = in_group(g)
                firsts = [g + bc_, g + cc_] + [g * BG + xc + b for b in range(BG)] + [g * BG + zc + b for b in range(BG)]
                for k, j in enumerate(firsts):
                    load(piece(k), blocks[:, :, bass.ds(j, 1), :].rearrange("p k j c -> p k (j c)"))
                for b in range(BG):
                    load(piece(NCB + BG + b), rows[:, bass.ds(g * BG + b, 1), :].rearrange("p j n -> p (j n)"))
            with sp.Fori(0, G - 1) as g:
                ssd_group(g)
            ssd_group(G - 1)
            ffn(1)

        @block.gpsimd
        def _(pool):
            pool.memset(ident[:, :], 0.0).then_inc(masks_ready, 1)
            pool.memset(f(tri[:, :]), 1.0).then_inc(masks_ready, 1)
            pool.memset(f(ones[:, :]), 1.0).then_inc(masks_ready, 1)
            pool.memset(masks[:, 1, :], 0.0).then_inc(masks_ready, 1)
            pool.memset(masks[:, 0, P:2 * P], 0.0).then_inc(masks_ready, 1)
            pool.memset(one_col, 1.0).then_inc(masks_ready, 1)
            pool.memset(eps[:, :], EPS).then_inc(masks_ready, 1)
            pool.memset(masks[:, 0, 0:P], NEG).then_inc(masks_ready, 1)
            for j in range(PAD):
                pool.memset(inv_count[:, j:j + 1], 1.0 / (j + 1)).then_inc(masks_ready, 1)
            pool.wait_ge(masks_ready, 8 + PAD)
            pool.affine_select(out=ident[:, :], in_=ident[:, :], compare_op=ALU.not_equal, fill=1.0, base=0,
                               pattern=[[-1, P]], channel_multiplier=1).then_inc(masks_ready, 1)
            pool.affine_select(out=tri[:, :], in_=f(tri[:, :]), compare_op=ALU.is_ge, fill=0.0, base=0,
                               pattern=[[1, P]], channel_multiplier=-1).then_inc(masks_ready, 1)
            pool.affine_select(out=masks[:, 1, 0:P], in_=masks[:, 1, 0:P], compare_op=ALU.is_ge, fill=NEG, base=-1,
                               pattern=[[1, P]], channel_multiplier=-1).then_inc(masks_ready, 1)
            for m in range(2):
                pool.affine_select(out=masks[:, m, P:2 * P], in_=masks[:, m, P:2 * P], compare_op=ALU.is_ge, fill=NEG,
                                   base=0, pattern=[[-1, P]], channel_multiplier=1).then_inc(masks_ready, 1)

            def lo(piece):
                pool.wait_ge(hi_done, piece.count(1))
                pool.tensor_tensor(w_lo[piece.slot][:, :], raw[piece.raw][:, :], f(w_hi[piece.slot][:, :]),
                                   ALU.subtract).then_inc(lo_done, 1)

            for n in range(10 + LEAD):
                lo(Piece(n))

            for j in range(2 * NT):
                pool.wait_ge(rsum_ready, j + 1)
                pr = prob[j % 3]
                pool.tensor_tensor(pr[:, :, :], pr[:, :, :],
                                   row_sum[j % 3].unsqueeze(2).to_broadcast([P, QH, 2 * P]), ALU.mult)\
                    .then_inc(p_normed, 1)
                if j in (2, 3):
                    lo(Piece(12 + j))
            for n in range(10 + LEAD + 2, NA):
                lo(Piece(n))

            def ffn(layer):
                with pool.Fori(0, ROUNDS) as i:
                    for k in range(RP):
                        lo(Piece(FFN_AT[layer] + k, i, RP, ROUNDS))

            ffn(0)
            pool.wait_ge(wdt_hi_done, 1)
            pool.tensor_tensor(wdt_lo[:, :, :], wdt[:, :, :], f(wdt_hi[:, :, :]), ALU.subtract).then_inc(wdt_split, 1)
            t = Tally(chunk=0, carry=0, sq=0, added=0)

            def ssd_group(g):
                piece = in_group(g)
                for k in range(NCB + 3):
                    lo(piece(k))
                for c in range(NT):
                    def heads(ap):
                        return ap[:, :].rearrange("p (h d) -> p h d", d=PH)

                    def factor(first):
                        return gc[:, first + c * HG:first + (c + 1) * HG].unsqueeze(2).to_broadcast([P, HG, PH])
                    pool.wait_ge(xdt_ready, t.count("chunk", c + 1))
                    if c:
                        pool.wait_ge(states_full, t.count("chunk", c))
                    pool.tensor_tensor(heads(xds), heads(xdt[c % 2]), factor(GC_DS), ALU.mult).then_inc(xds_ready, 1)
                    if c:
                        pool.wait_ge(state_ready, t.count("chunk", c))
                        pool.tensor_tensor(heads(decayed), heads(state), factor(GC_CD), ALU.mult)\
                            .then_inc(decayed_ready, 1)
                    if c in LO_AFTER_CHUNK:
                        lo(piece(LO_AFTER_CHUNK[c]))
                for h in range(2):
                    for b in range(1, BG):
                        pool.wait_ge(sq_ready, t.count("sq", BG * h + b + 1))
                        if b > 1:
                            pool.wait_ge(sq_added, t.count("added"))
                        ins = pool.tensor_tensor(sq[h][0][:, :], sq[h][0][:, :], sq[h][b][:, :], ALU.add)
                        if b < BG - 1:
                            ins.then_inc(sq_added, 1)
                            t.add("added")
                    ins.then_inc(sq_summed, 1)
                t.add("sq", 2 * BG)
                t.add("chunk", NT)
                t.add("carry", NT - 1)

            with pool.Fori(0, G - 1) as g:
                t.enter(g, chunk=NT, carry=NT - 1, sq=2 * BG, added=2 * (BG - 2))
                ssd_group(g)
                t.leave(G - 1)
            ssd_group(G - 1)
            ffn(1)

        @block.scalar
        def _(act):
            def load_norm_w(w):
                act.dma_start(norm_w[:, :], w.rearrange("(a n) -> a n", a=1).to_broadcast([P, DM]))\
                    .then_inc(norm_w_loaded, 16)

            load_norm_w(mix_norm_w[0])
            for tt in range(NT):
                act.dma_start(xres[:, tt, :], x[0, tt * P:(tt + 1) * P, :]).then_inc(x_loaded[tt], 16)

            t = Tally(unit=0, out=0, tile=0, chunk=0, half=0, conv=0, z=0, gu=0, tail=0, group=0, ssq=0)

            def hi(piece, free=None, count=None):
                if free is not None:
                    act.wait_ge(free, count)
                act.wait_ge(raw_ready[piece.raw], piece.raw_count())
                act.activation(w_hi[piece.slot][:, :], raw[piece.raw][:, :], ACT.Copy).then_inc(hi_done, 1)

            def square(tt, waste=junk):
                act.activation(waste[:, :], xres[:, tt, :], ACT.Square, accum_out=ssq[:, tt:tt + 1]).then_inc(ssq_ready, 1)
                t.add("tile")
                act.wait_ge(ssq_ready, t.count("tile"))
                act.activation(std[:, tt:tt + 1], ssq[:, tt:tt + 1], ACT.Sqrt, scale=1.0 / DM, bias=eps[:, :])\
                    .then_inc(std_ready, 1)

            def norm(wait_tile, beside={}, waste=junk, tail=NT - 2):
                unit0 = t.n["unit"]

                def xhi(tt):
                    if tt < tail:
                        act.wait_ge(pair_full, unit0 + tt + 1)
                        src = pair(unit0 + tt)
                    else:
                        act.wait_ge(tail_full, t.count("tail", 1))
                        src = tail_pair(tt)
                        t.add("tail")
                    act.activation(xn_hi[:, :, tt * P:(tt + 1) * P], src.rearrange("p a (b c) -> p (a b) c", c=P), ACT.Copy)\
                        .then_inc(xn_hi_done, 1)
                for tt in range(NT):
                    wait_tile(tt)
                    square(tt, waste)
                    if tt in beside:
                        hi(beside[tt])
                    if tt >= 3:
                        xhi(tt - 3)
                for tt in range(NT - 3, NT):
                    xhi(tt)
                t.add("unit", tail)

            act.wait_ge(masks_ready, PAD + 13)
            hi(Piece(0))
            norm(lambda tt: act.wait_ge(x_loaded[tt], 16), {2: Piece(1), 4: Piece(2), 6: Piece(3)}, tail=NT // 2)

            for k in range(10):
                t.add("unit", 2 if k == 7 else 1)
                hi(Piece(k + LEAD), pair_full, t.count("unit"))

            act.wait_ge(const_ready, 1)
            for b in range(4):
                act.wait_ge(pair_full, t.count("unit", 1))
                act.activation(xn_hi[:, 4 + b, :], flat(pair(t.n["unit"])), ACT.Copy, scale=p_scale[:, b:b + 1])\
                    .then_inc(cat_hi_done, 1)
                t.add("unit")

            NJ = 2 * NT

            def exps(j):
                act.wait_ge(max_ready, j + 1)
                r = j % 3
                for h in range(QH):
                    act.activation(prob[r][:, h, :], prob[r][:, h, :], ACT.Exp, bias=neg_max[r][:, h:h + 1],
                                   accum_out=row_sum[r][:, h:h + 1])
                act.activation(sink_exp[r], sink_exp[r], ACT.Exp).then_inc(p_ready, 1)

            def v_hi(j):
                rows = slice(64 * (j % 2), 64 * (j % 2) + 64)
                act.wait_ge(v_full, j + 1)
                act.activation(xn_hi[rows, 0:QH, (j // 2) * P:(j // 2 + 1) * P],
                               ps[rows, 6, :].rearrange("p (h q) -> p h q", q=P), ACT.Copy).then_inc(cat_hi_done, 1)

            exps(0)
            exps(1)
            for j in range(NJ):
                if j >= 1:
                    v_hi(j - 1)
                act.wait_ge(t_full, j + 1)
                act.activation(probT[:, :, :, :].rearrange("p a b c -> p (a b c)"),
                               ps[:, 4:6, :].rearrange("p a b -> p (a b)"), ACT.Copy).then_inc(pT_ready, 1)
                if j + 2 < NJ:
                    exps(j + 2)
                if j < 2:
                    hi(Piece(10 + LEAD + j))
            v_hi(NJ - 1)
            t.add("unit", NJ)
            load_norm_w(ffn_norm_w[0])
            for n in range(12 + LEAD, NA + 2):
                hi(Piece(n), po_full, NJ)

            def norm_after_outs(beside={}, waste=junk):
                o = t.n["out"]
                norm(lambda tt: act.wait_ge(out_added, o + 2 * tt + 2), beside, waste)
                t.add("out", 2 * NT)

            norm_after_outs()
            for n in (NA + 2, NA + 3):
                hi(Piece(n))

            def gate_up(n0, i, turns):
                for b in range(FB):
                    hi(Piece(n0 + 4 + b, i, RP, turns), out_full, t.count("out"))
                for k in range(2 * FB):
                    act.wait_ge(pair_full, t.count("unit", 1))
                    act.activation(gate[k % 2][:, :], pair(t.n["unit"])[:, 0, :], ACT.Silu).then_inc(gate_done, 1)
                    act.wait_ge(pair_freed, t.count("unit", 1))
                    act.activation(h_hi[:, k // 2, (k % 2) * BANK:(k % 2 + 1) * BANK], hid[k % 2][:, :], ACT.Copy)\
                        .then_inc(h_hi_done, 1)
                    t.add("gu")
                    t.add("unit")

            def ffn(layer):
                n0 = FFN_AT[layer]
                gate_up(n0, None, 1)
                with act.Fori(0, ROUNDS - 1) as i:
                    t.enter(i, unit=2 * FB, gu=2 * FB, out=2 * NT)
                    for k in range(LEAD):
                        hi(Piece(n0 + RP + k, i, RP, ROUNDS - 1))
                    t.add("out", 2 * NT)
                    gate_up(n0 + RP, i, ROUNDS - 1)
                    t.leave(ROUNDS - 1)

            act.wait_ge(xn_ready, 2 * NT)
            load_norm_w(mix_norm_w[1])
            act.dma_start(wdt[:, :, :], ssd_w_in[0][:, dtc:dtc + SH].rearrange("(k p) c -> p k c", p=P))\
                .then_inc(wdt_loaded, 16)
            ffn(0)
            act.wait_ge(wdt_loaded, 16)
            act.activation(wdt_hi[:, :, :], wdt[:, :, :], ACT.Copy).then_inc(wdt_hi_done, 1)
            hi(Piece(SSD0))
            norm_after_outs({k: Piece(SSD0 + k) for k in range(1, LEAD)})

            act.wait_ge(dts_v, 1)
            act.activation(D[2][:, :, :], D[1][:, :, :], ACT.Exp, scale=-1.0).then_inc(dts_a, 1)
            act.activation(exp_a, exp_a, ACT.Exp).then_inc(dts_a, 1)
            act.wait_ge(dts_v, 2)
            act.activation(D[4][:, :, :], D[3][:, :, :], ACT.Ln).then_inc(dts_a, 1)
            act.wait_ge(dts_v, 3)
            act.activation(gda_hi[:, :, :].rearrange("p g (c h) -> p g c h", h=HG),
                           D[6][:, :, :].rearrange("p c (g h) -> p g c h", h=HG), ACT.Copy).then_inc(dts_a, 1)
            act.wait_ge(dts_v, 5)
            for d, first in ((D[3], GC_DS), (D[7], GC_CD)):
                act.activation(gconst[:, :, first:first + NT * HG],
                               d[:, :, :].rearrange("p c s -> p (c s)").rearrange("p (g k) -> p g k", g=G), ACT.Exp)\
                    .then_inc(dts_a, 1)
            t.add("unit")

            def ssd_group(g, last=False):
                piece = in_group(g)
                hi(piece(LEAD))
                act.wait_ge(gc_ready, t.count("group", 1))
                for k in range(NCB):
                    act.wait_ge(pair_full, t.count("unit", 1))
                    act.activation(acc[k % 2][:, :], flat(pair(t.n["unit"])), ACT.Identity,
                                   scale=gc[:, GC_TAP + k * CONV + CONV - 1:GC_TAP + k * CONV + CONV],
                                   bias=gc[:, GC_BIAS + k:GC_BIAS + k + 1]).then_inc(acc_ready, 1)
                    if k < 4:
                        hi(piece(LEAD + 1 + k))
                    act.wait_ge(pair_freed, t.count("unit", 1))
                    dst = (BT[:, :], CT[:, :])[k] if k < 2 else yx[:, k - 2, :]
                    act.activation(dst, acc[k % 2][:, :], ACT.Silu).then_inc(silu_done, 1)
                    t.add("unit")
                    t.add("conv")

                def silu_z(n):
                    act.wait_ge(z_full, t.count("z", n + 1))
                    act.activation(zs[n][:, :] if n < BG else ps[:, Z_BANK, :], ps[:, Z_BANK, :], ACT.Silu)\
                        .then_inc(z_done, 1)

                for c in range(NT):
                    for hf in range(2):
                        act.wait_ge(bc_full, t.count("half", 1))
                        bc = ps[:, DECAY + hf, :].rearrange("p (h l) -> p h l", l=P)
                        if hf == 0 and c >= 2:
                            act.wait_ge(y_ready, t.count("chunk", c - 1))
                        for odd in range(2):
                            rows = slice(64 * odd, 64 * odd + 64)
                            ins = act.activation(eacs[c % 2][rows, 2 * hf:2 * hf + 2, :], bc[rows, odd::2, :], ACT.Exp)
                        ins.then_inc(e_ready, 1)
                        act.wait_ge(e_ready, t.count("half", 1))
                        for h in range(4):
                            col = GC_ACS + c * HG + 4 * hf + h
                            ins = act.activation(bc[:, h, :], bc[:, h, :], ACT.Relu, scale=-1.0, bias=gc[:, col:col + 1])
                        ins.then_inc(relu_done, 1)
                        t.add("half")
                        act.wait_ge(relu_done, t.count("half"))
                        act.activation(bc, bc, ACT.Exp, scale=-1.0).then_inc(dec_ready, 1)
                    if c < NT - 1:
                        silu_z(c)
                    if c in HI_AFTER_CHUNK:
                        hi(piece(HI_AFTER_CHUNK[c]))
                t.add("chunk", NT)

                def split(b, h):
                    act.activation(sq[h][b][:, :], yx[:, b, h * BANK:(h + 1) * BANK], ACT.Square).then_inc(sq_ready, 1)
                    act.activation(y_hi[:, b, h * BANK:(h + 1) * BANK], yx[:, b, h * BANK:(h + 1) * BANK], ACT.Copy,
                                   scale=gc[:, GC_NW + b:GC_NW + b + 1]).then_inc(y_hi_done, 1)

                def root(h):
                    act.wait_ge(ssq_full, t.count("ssq", h + 1))
                    act.activation(rms[:, 4 * h:4 * h + 4], ps[:, CB + h, 0:4], ACT.Sqrt, scale=1.0 / (BG * P),
                                   bias=eps[:, :]).then_inc(rms_rooted, 1)

                act.wait_ge(ydiag_full, t.count("chunk"))
                act.wait_ge(z_gated, t.count("z", BG - 1))
                for b in range(BG - 1):
                    split(b, 0)
                silu_z(2 * BG - 1)
                act.wait_ge(z_gated, t.count("z", BG))
                split(BG - 1, 0)
                hi(piece(GP))
                root(0)
                for b in range(BG):
                    act.wait_ge(z_gated, t.count("z", BG + 1 + b))
                    split(b, 1)
                if last:
                    act.dma_start(norm_w3[:, :], ffn_norm_w[1].rearrange("(a n) -> a n", a=1).to_broadcast([P, DM]))\
                        .then_inc(norm_w_loaded, 16)
                root(1)
                t.add("z", 2 * BG)
                t.add("group")
                t.add("ssq", 2)
                if last:
                    norm_after_outs({NT - 1: piece(GP + 1)}, junk3)
                    for k in range(2, LEAD):
                        hi(piece(GP + k))
                else:
                    t.add("out", 2 * NT)
                    for k in range(1, LEAD):
                        hi(piece(GP + k), out_full, t.count("out"))

            with act.Fori(0, G - 1) as g:
                t.enter(g, unit=NCB, conv=NCB, z=2 * BG, chunk=NT, half=2 * NT, out=2 * NT, group=1,
                        ssq=2)
                ssd_group(g)
                t.leave(G - 1)
            ssd_group(G - 1, True)

            act.wait_ge(xn_ready, 4 * NT)
            load_norm_w(final_norm_w)
            ffn(1)
            o = t.n["out"]

            def store(tt):
                act.wait_ge(final_ready, tt + 1)
                act.dma_start(out[0, tt * P:(tt + 1) * P, :], xn[tt % 2][:, :]).then_inc(stored[tt % 2], 16)
            for tt in range(NT):
                act.wait_ge(out_added, o + 2 * tt + 2)
                square(tt)
                if tt:
                    store(tt - 1)
            store(NT - 1)
            for i in range(2):
                act.wait_ge(stored[i], 16 * NT // 2)

        @block.tensor
        def _(pe):
            t = Tally(unit=0, out=0, tile=0, conv=0, z=0, gu=0, chunk=0, half=0, carry=0, tail=0,
                      rms=0)

            def mm3(dst, l_hi, l_lo, r_hi, r_lo, first, last):
                pe.matmul(dst, l_hi, r_hi, start=first, stop=False)
                pe.matmul(dst, l_hi, r_lo, start=False, stop=False)
                return pe.matmul(dst, l_lo, r_hi, start=False, stop=last)

            def begin_unit():
                if t.i is not None or t.n["unit"] >= 2:
                    pe.wait_ge(pair_freed, t.count("unit", -1))
                p = pair(t.n["unit"])
                t.add("unit")
                return p

            def begin_out():
                if t.i is not None or t.n["out"] >= 4:
                    pe.wait_ge(out_added, t.count("out", -3))
                bank = ps[:, 4 + t.n["out"] % 4, :]
                t.add("out")
                return bank

            def norm_T(tt, xn=xn, tail=False):
                pe.wait_ge(xn_ready, t.count("tile", 1))
                if tail:
                    if t.n["tail"] >= 2:
                        pe.wait_ge(tail_split, t.count("tail", -1))
                    p, full = tail_pair(tt), tail_full
                    t.add("tail")
                else:
                    p, full = begin_unit(), pair_full
                p = p.rearrange("p a (b c) -> p (a b) c", c=P)
                for k in range(NK):
                    ins = pe.transpose(p[:, k, :], xn[tt % 2][:, k * P:(k + 1) * P], ident[:, :])
                ins.then_inc(full, 1)
                t.add("tile")

            def tail_T(xn=xn):
                pe.wait_ge(out_added, t.count("out"))
                norm_T(NT - 2, xn, True)
                norm_T(NT - 1, xn, True)

            def all_normed():
                pe.wait_ge(tail_split, t.count("tail"))
                pe.wait_ge(pair_freed, t.count("unit", -1))

            def split_of(piece):
                return [w[piece.slot][:, :].rearrange("p (k c) -> p k c", c=P) for w in (w_hi, w_lo)]

            def columns(dst, piece, half):
                p_hi, p_lo = split_of(piece)
                tok = slice(half * BANK, (half + 1) * BANK)
                for k in range(NK):
                    ins = mm3(dst, p_hi[:, k, :], p_lo[:, k, :], xn_hi[:, k, tok], xn_lo[:, k, tok],
                              k == 0, k == NK - 1)
                return ins

            def project(piece):
                pe.wait_ge(lo_done, piece.count(1))
                p = begin_unit()
                columns(p[:, 0, :], piece, 0)
                columns(p[:, 1, :], piece, 1).then_inc(pair_full, 1)

            def rows(bank, n, parts):
                tok, col = slice(n // 2 * P, (n // 2 + 1) * P), slice(n % 2 * BANK, (n % 2 + 1) * BANK)
                for k, (a_hi, a_lo, slot) in enumerate(parts):
                    ins = mm3(bank, a_hi[:, tok], a_lo[:, tok], w_hi[slot][:, col], w_lo[slot][:, col],
                              k == 0, k == len(parts) - 1)
                return ins

            def outputs(parts, with_norm=False, before=None):
                for n in range(2 * NT):
                    if before:
                        before(n)
                    rows(begin_out(), n, parts).then_inc(out_full, 1)
                    if with_norm and n % 2 and n // 2 >= 2:
                        norm_T(n // 2 - 2)

            pe.wait_ge(masks_ready, 13 + PAD)
            for tt in range(NT // 2):
                norm_T(tt)
            firsts = []
            for k in range(2):
                pe.wait_ge(lo_done, k + 1)
                firsts.append(begin_unit())
                if k == 0:
                    pe.wait_ge(pair_freed, NT // 2)
                columns(firsts[k][:, 0, :], Piece(k), 0)
                for tt in range(NT // 2 + 2 * k, NT // 2 + 2 * k + 2):
                    norm_T(tt, tail=True)
            pe.wait_ge(tail_split, NT // 2)
            pe.wait_ge(const_loaded, 16 * 9)
            NB = CC // P
            pe.transpose(ps[:, 4, 0:(CONV + 1) * NB], stage[0:(CONV + 1) * NB, 0, :], ident[0:(CONV + 1) * NB, 0:(CONV + 1) * NB])
            pe.transpose(ps[:, 4, P:P + G * BG + 4], stage[0:G * BG + 4, 1, :], ident[0:G * BG + 4, 0:G * BG + 4])\
                .then_inc(const_T, 1)
            for k in range(2):
                columns(firsts[k][:, 1, :], Piece(k), 1).then_inc(pair_full, 1)

            for k in range(2, 10):
                project(Piece(k))
                if k == 6:
                    v_units = t.count("unit", -1)
                    pe.wait_ge(pair_freed, v_units)
                    p = begin_unit().rearrange("p a (b c) -> p (a b) c", c=P)
                    for tt in range(NT):
                        ins = pe.transpose(p[:, tt, :], v_ch[:, tt * P:(tt + 1) * P], ident[:, :])
                    ins.then_inc(pair_full, 1)

            pe.wait_ge(d_ready, 4)
            for b in range(4):
                p = begin_unit()
                for half in range(2):
                    ins = pe.matmul(p[:, half, :], pool_wt[:, b, :], u[b][:, PAD + half * BANK:PAD + (half + 1) * BANK],
                                    start=True, stop=True)
                ins.then_inc(pair_full, 1)

            NJ = 2 * NT

            def scores(j):
                n, kv = j // 2, j % 2
                hd = slice(64 * kv, 64 * kv + 64)
                p = begin_unit().rearrange("p a (b c) -> p (a b) c", c=2 * P)
                for h in range(QH):
                    ins = pe.matmul(p[:, h, :], qT[hd, h, n * P:(n + 1) * P], kT[hd, n * P:(n + 2) * P],
                                    start=True, stop=True)
                ins.then_inc(pair_full, 1)

            pooled = [(xn_hi[:, 4 + b, :], xn_lo[:, 4 + b, :], Piece(10 + b).slot) for b in range(4)]
            def pooled_out(j):
                if j:
                    pe.wait_ge(po_added, j)
                rows(ps[:, 7, :], j, pooled).then_inc(po_full, 1)

            scores(0)
            scores(1)
            pe.wait_ge(lo_done, 14)
            pooled_out(0)
            for j in range(NJ):
                n, kv = j // 2, j % 2
                if j + 2 < NJ:
                    scores(j + 2)
                pe.wait_ge(p_normed, j + 1)
                if j:
                    pe.wait_ge(pT_ready, j)
                pT = ps[:, 4:6, :].rearrange("p a (h q) -> p a h q", q=P)
                for kt in range(2):
                    for h in range(QH):
                        ins = pe.transpose(pT[:, kt, h, :], prob[j % 3][:, h, kt * P:(kt + 1) * P], ident[:, :])
                ins.then_inc(t_full, 1)
                if j + 1 < NJ:
                    pooled_out(j + 1)
                pe.wait_ge(pT_ready, j + 1)
                if j:
                    pe.wait_ge(cat_done, j)
                for kt in range(2):
                    ins = pe.matmul(ps[64 * kv:64 * kv + 64, 6, :], vt[:, n + kt, 64 * kv:64 * kv + 64],
                                    probT[:, kt, :, :].rearrange("p h q -> p (h q)"), start=kt == 0, stop=kt == 1)
                ins.then_inc(v_full, 1)

            pe.wait_ge(lo_done, NA)
            pe.wait_ge(cat_done, NJ)
            pe.wait_ge(po_added, NJ)
            outputs([(xn_hi[:, b, :], xn_lo[:, b, :], Piece(14 + b).slot) for b in range(4)], with_norm=True)

            def gate_up(n0, i, turns, tail_xn=None):
                for b in range(FB):
                    gu = [Piece(n0 + 2 * b + m, i, RP, turns) for m in range(2)]
                    pe.wait_ge(lo_done, gu[1].count(1))
                    for half in range(2):
                        p = begin_unit()
                        columns(p[:, 0, :], gu[0], half)
                        if tail_xn and b == half == 0:
                            tail_T(tail_xn)
                        columns(p[:, 1, :], gu[1], half).then_inc(pair_full, 1)
                        t.add("gu")
                        if tail_xn and b == half == 0:
                            all_normed()

            def down(n0, i, turns, with_norm=False):
                pe.wait_ge(lo_done, Piece(n0 + 5, i, RP, turns).count(1))

                def hidden_split(n):
                    if n % NT == 0:
                        pe.wait_ge(h_split, t.count("gu", n // NT - 1))
                outputs([(h_hi[:, b, :], h_lo[:, b, :], 4 + b) for b in range(FB)], with_norm, hidden_split)

            def ffn(layer, with_norm, tail_xn):
                n0 = FFN_AT[layer]
                gate_up(n0, None, 1, tail_xn)
                with pe.Fori(0, ROUNDS - 1) as i:
                    t.enter(i, unit=2 * FB, gu=2 * FB, out=2 * NT)
                    down(n0, i, ROUNDS - 1)
                    gate_up(n0 + RP, i, ROUNDS - 1)
                    t.leave(ROUNDS - 1)
                down(n0 + RP * (ROUNDS - 1), None, 1, with_norm)

            ffn(0, True, xn)

            pe.wait_ge(wdt_split, 1)
            p = begin_unit()
            dt_units = t.count("unit")

            def dt_rows(half):
                tok = slice(half * BANK, (half + 1) * BANK)
                for k in range(NK):
                    ins = mm3(p[0:SH, half, :], wdt_hi[:, k, :], wdt_lo[:, k, :], xn_hi[:, k, tok], xn_lo[:, k, tok],
                              k == 0, k == NK - 1)
                return ins
            dt_rows(0)
            tail_T()
            all_normed()
            dt_rows(1).then_inc(pair_full, 1)
            pe.wait_ge(lo_done, SSD0 + 1)
            b_unit = begin_unit()
            columns(b_unit[:, 0, :], Piece(SSD0), 0)
            pe.wait_ge(pair_freed, dt_units)
            for tt in range(NT):
                ins = pe.transpose(ps[:, 4, tt * SH:(tt + 1) * SH], dtT[0:SH, tt * P:(tt + 1) * P], ident[0:SH, 0:SH])
            ins.then_inc(dt_full, 1)
            columns(b_unit[:, 1, :], Piece(SSD0), 1).then_inc(pair_full, 1)
            pe.wait_ge(lo_done, SSD0 + 2)
            c_unit = begin_unit()
            columns(c_unit[:, 0, :], Piece(SSD0 + 1), 0)
            pe.wait_ge(dts_v, 4)
            for m, w in enumerate((tri, ones)):
                for n, d in enumerate((gda_hi, gda_lo)):
                    ins = pe.matmul(ps[:, 5 + m, 0:G * NT * HG], w[:, :], d[:, :, :].rearrange("p g k -> p (g k)"),
                                    start=n == 0, stop=n == 1)
            ins.then_inc(sums_full, 1)
            columns(c_unit[:, 1, :], Piece(SSD0 + 1), 1).then_inc(pair_full, 1)

            def ssd_group(g, last=False):
                piece = in_group(g)
                for k in range(2, NCB):
                    project(piece(k))
                t.add("conv", NCB)

                def z_unit(n):
                    if n < BG:
                        pe.wait_ge(lo_done, piece(NCB + n).count(1))
                    if 1 <= n <= BG:
                        pe.wait_ge(z_done, t.count("z", n))
                    elif n > BG:
                        pe.wait_ge(z_gated, t.count("z", n - BG))
                    columns(ps[:, Z_BANK, :], piece(NCB + n % BG), int(n < BG)).then_inc(z_full, 1)

                def token_major(c):
                    tok = slice(c * P, (c + 1) * P)
                    if c:
                        pe.wait_ge(cb_freed, t.count("chunk", c))
                    pe.matmul(ps[:, CB, 0:P], BT[:, tok], CT[:, tok], start=True, stop=True)
                    pe.transpose(ps[:, CB, P:2 * P], BT[:, tok], ident[:, :]).then_inc(cb_full, 1)
                    if c:
                        pe.wait_ge(xdt_ready, t.count("chunk", c))
                    for b in range(BG):
                        ins = pe.transpose(ps[:, XS, b * P:(b + 1) * P], yx[:, b, tok], ident[:, :])
                    ins.then_inc(xsT_full, 1)

                def decay_sums(c):
                    for hf in range(2):
                        if c:
                            pe.wait_ge(m_ready, t.count("half", 2 * c + hf - 1))
                        for h in range(4):
                            for n, d in enumerate((da_hi, da_lo)):
                                col = c * HG + 4 * hf + h
                                ins = pe.matmul(ps[:, DECAY + hf, h * P:(h + 1) * P],
                                                d[:, col:col + 1].to_broadcast([P, P]), tri[:, :], start=n == 0, stop=n == 1)
                        ins.then_inc(bc_full, 1)

                pe.wait_ge(out_added, t.count("out"))
                z_unit(0)
                pe.wait_ge(pair_freed, t.count("unit", -1))
                decay_sums(0)
                pe.wait_ge(silu_done, t.count("conv"))
                token_major(0)
                for c in range(NT):
                    tok = slice(c * P, (c + 1) * P)
                    if c + 1 < NT:
                        token_major(c + 1)
                    pe.wait_ge(xds_ready, t.count("chunk", c + 1))
                    if c:
                        pe.wait_ge(state_ready, t.count("chunk", c))
                    pe.matmul(ps[:, STATES, :], btok[:, :], xds[:, :], start=True, stop=True).then_inc(states_full, 1)
                    if c:
                        pe.wait_ge(yoff_read, t.count("chunk", c))
                        for b in range(BG):
                            ins = pe.matmul(ps[:, YOFF, b * P:(b + 1) * P], state[:, b * P:(b + 1) * P], CT[:, tok],
                                            start=True, stop=True)
                        ins.then_inc(yoff_full, 1)
                    if c + 1 < NT:
                        decay_sums(c + 1)
                    pe.wait_ge(m_ready, t.count("half", 2 * c + 2))
                    if c:
                        pe.wait_ge(y_ready, t.count("chunk", c))
                    for h in range(HG):
                        ins = pe.matmul(ps[64 * (h % 2):64 * (h % 2) + 64, YDIAG, (h // 2) * P:(h // 2 + 1) * P],
                                        xdt[c % 2][:, h * PH:(h + 1) * PH], mdec[:, h, :], start=True, stop=True)
                    ins.then_inc(ydiag_full, 1)
                    if c < NT - 2:
                        z_unit(c + 1)
                    elif c == NT - 1:
                        z_unit(NT - 1)
                t.add("chunk", NT)
                t.add("half", 2 * NT)
                t.add("carry", NT - 1)

                def square_sums(h):
                    pe.wait_ge(sq_summed, t.count("rms", h + 1))
                    for tt in range(NT // 2):
                        ins = pe.matmul(ps[:, CB + h, tt:tt + 1], sq[h][0][:, tt * P:(tt + 1) * P], one_col,
                                        start=True, stop=True)
                    ins.then_inc(ssq_full, 1)

                for n in range(2 * NT):
                    tok, col = slice(n // 2 * P, (n // 2 + 1) * P), slice(n % 2 * BANK, (n % 2 + 1) * BANK)
                    if n == NT:
                        pe.wait_ge(y_split, t.count("z", 2 * BG))
                    for b in range(BG):
                        if n == 0:
                            pe.wait_ge(y_split, t.count("z", b + 1))
                            pe.wait_ge(lo_done, piece(NCB + BG + b).count(1))
                        if b == 0:
                            bank = begin_out()
                        s = ssd_slots[NCB + BG + b]
                        ins = mm3(bank, y_hi[:, b, tok], y_lo[:, b, tok], w_hi[s][:, col], w_lo[s][:, col],
                                  b == 0, b == BG - 1)
                    ins.then_inc(out_full, 1)
                    if n in SSQ_AFTER_OUT:
                        square_sums(SSQ_AFTER_OUT.index(n))
                    if last and n % 2 and n // 2 >= 2:
                        norm_T(n // 2 - 2, xn3)
                t.add("z", 2 * BG)
                t.add("rms", 2)
                if not last:
                    for k in range(2):
                        project(piece(GP + k))

            with pe.Fori(0, G - 1) as g:
                t.enter(g, unit=NCB, conv=NCB, z=2 * BG, chunk=NT, half=2 * NT, out=2 * NT, carry=NT - 1, rms=2)
                ssd_group(g)
                t.leave(G - 1)
            ssd_group(G - 1, True)

            ffn(1, False, xn3)

        @block.vector
        def _(dve):
            t = Tally(unit=0, out=0, tile=0, conv=0, z=0, gu=0, chunk=0, half=0, carry=0, group=0, rms=0, tail=0,
                      step=0)

            def step(ins):
                ins.then_inc(step_done, 1)
                t.add("step")
                dve.wait_ge(step_done, t.count("step"))

            def unit(full=True):
                if full:
                    dve.wait_ge(pair_full, t.count("unit", 1))
                return flat(pair(t.n["unit"]))

            def freed(ins):
                ins.then_inc(pair_freed, 1)
                t.add("unit")

            def add_out(scale=None):
                n = t.n["out"] % (2 * NT)
                tt, half = n // 2, n % 2
                bank = ps[:, 4 + n % 4, :]
                dve.wait_ge(out_full, t.count("out", 1))
                if t.i is not None or t.n["out"] >= 2 * NT:
                    dve.wait_ge(out_added, t.count("out", 1 - 2 * NT))
                dst = xres[:, tt, half * BANK:(half + 1) * BANK]
                if scale is None:
                    ins = dve.tensor_tensor(dst, bank, dst, ALU.add)
                else:
                    ins = dve.scalar_tensor_tensor(dst, bank, scale[:, tt:tt + 1], dst, ALU.mult, ALU.add)
                ins.then_inc(out_added, 1)
                t.add("out")

            def normed(n_norm, tt, dst, norm_w=norm_w):
                dve.wait_ge(std_ready, NT * n_norm + tt + 1)
                dve.reciprocal(rstd[:, tt:tt + 1], std[:, tt:tt + 1]).then_inc(rstd_ready, 1)
                dve.wait_ge(rstd_ready, NT * n_norm + tt + 1)
                if tt == 0:
                    dve.wait_ge(norm_w_loaded, 16 * (n_norm + 1))
                return dve.scalar_tensor_tensor(dst[:, :], xres[:, tt, :], rstd[:, tt:tt + 1], norm_w[:, :],
                                                ALU.mult, ALU.mult)

            def norm(n_norm, outs=None, xn=xn, norm_w=norm_w, tail=NT - 2):
                unit0, tail0 = t.n["unit"], t.n["tail"]

                def make(tt):
                    if tt - 2 >= tail:
                        dve.wait_ge(tail_full, tail0 + tt - 1 - tail)
                    elif tt >= 2:
                        dve.wait_ge(pair_full, unit0 + tt - 1)
                    normed(n_norm, tt, xn[tt % 2], norm_w).then_inc(xn_ready, 1)

                def lo(tt):
                    dve.wait_ge(xn_hi_done, NT * n_norm + tt + 1)
                    tok = slice(tt * P, (tt + 1) * P)
                    src = pair(unit0 + tt) if tt < tail else tail_pair(tt)
                    ins = dve.tensor_tensor(xn_lo[:, :, tok], src.rearrange("p a (b c) -> p (a b) c", c=P),
                                            f(xn_hi[:, :, tok]), ALU.subtract)
                    if tt < tail:
                        freed(ins)
                    else:
                        ins.then_inc(tail_split, 1)
                        t.add("tail")
                for tt in range(NT):
                    if outs:
                        outs(tt)
                    if tt >= 1:
                        make(tt - 1)
                    if tt >= 3:
                        lo(tt - 3)
                make(NT - 1)
                for tt in range(NT - 3, NT):
                    lo(tt)

            def two_outs(tt):
                add_out()
                add_out()

            dve.wait_ge(masks_ready, 13 + PAD)
            norm(0, tail=NT // 2)
            dve.wait_ge(const_T, 1)
            NB = CC // P
            c0, c1 = ps[:, 4, 0:(CONV + 1) * NB], ps[:, 4, P:P + G * BG + 4]
            for tap in range(CONV + 1):
                for k in range(2):
                    j = tap * NB + INNER // P + k * G
                    col = GC_TAP + k * CONV + tap if tap < CONV else GC_BIAS + k
                    dve.tensor_copy(gconst[:, :, col], c0[:, j:j + G])
                for b in range(BG):
                    col = GC_TAP + (2 + b) * CONV + tap if tap < CONV else GC_BIAS + 2 + b
                    dve.tensor_copy(gconst[:, :, col], c0[:, tap * NB + b:tap * NB + G * BG:BG])
            dve.tensor_copy(gconst[:, :, GC_NW:GC_NW + BG], c1[:, 0:G * BG].rearrange("p (g b) -> p g b", b=BG))
            for odd in range(2):
                hd = slice(64 * odd, 64 * odd + 64)
                dve.tensor_copy(gconst[hd, :, GC_D:GC_D + BG],
                                rep[hd, odd::2].rearrange("p (g b) -> p g b", b=BG))
            dve.tensor_scalar(neg_sink[:, :], sink, -1.0, None, ALU.mult)
            dve.tensor_copy(p_scale, c1[:, G * BG:G * BG + 4]).then_inc(const_ready, 1)

            for b in range(4):
                w = WINDOWS[b]
                dve.memset(u[b][:, 0:PAD], 0.0)
                if b == 0:
                    for i in range(2):
                        dve.memset(win[i][:, 0:PAD], 0.0)
                freed(dve.tensor_copy(u[b][:, PAD:], unit()))
                dve.wait_ge(pair_freed, t.count("unit"))
                src, shift, n = u[b], 1, 0
                while shift < w:
                    dst = win[n % 2]
                    step(dve.tensor_tensor(dst[:, PAD:], src[:, PAD:], src[:, PAD - shift:PAD + S - shift], ALU.add))
                    src, shift, n = dst, 2 * shift, n + 1
                step(dve.tensor_tensor(src[:, PAD:PAD + w], src[:, PAD:PAD + w], inv_count[:, 0:w], ALU.mult))
                dve.tensor_tensor(u[b][:, PAD:PAD + w], src[:, PAD:PAD + w], u[b][:, PAD:PAD + w], ALU.subtract)
                dve.scalar_tensor_tensor(u[b][:, PAD + w:], src[:, PAD + w:], 1.0 / w, u[b][:, PAD + w:],
                                         ALU.mult, ALU.subtract).then_inc(d_ready, 1)
            dve.wait_ge(d_ready, 4)
            dve.memset(kT[:, 0:P], 0.0)
            freed(dve.tensor_copy(kT[:, P:], unit()))
            freed(dve.tensor_copy(v_ch[:, :], unit()))
            dve.memset(vt[:, 0, :], 0.0)
            freed(dve.tensor_copy(qT[:, 0, :], unit()))
            freed(dve.tensor_copy(vt[:, 1:, :].rearrange("p a b -> p (a b)"), unit()))
            for i in range(1, 4):
                freed(dve.tensor_copy(qT[:, i, :], unit()))
            for b in range(4):
                dve.wait_ge(cat_hi_done, b + 1)
                freed(dve.scalar_tensor_tensor(xn_lo[:, 4 + b, :], unit(), p_scale[:, b:b + 1],
                                               f(xn_hi[:, 4 + b, :]), ALU.mult, ALU.subtract))

            NJ = 2 * NT

            def scores(j):
                n, kv, r = j // 2, j % 2, j % 3
                if j >= 3:
                    dve.wait_ge(t_full, j - 2)
                hd = slice(kv * QH, (kv + 1) * QH)
                m = masks[:, min(n, 1), :].unsqueeze(1).to_broadcast([P, QH, 2 * P])
                unit()
                freed(dve.scalar_tensor_tensor(prob[r][:, :, :],
                                               pair(t.n["unit"]).rearrange("p a (b c) -> p (a b) c", c=2 * P),
                                               float(HEAD_DIM) ** -0.5, m, ALU.mult, ALU.add))
                dve.wait_ge(pair_freed, t.count("unit"))
                step(dve.reduce_max(row_max[r], prob[r][:, :, :], AX_X))
                step(dve.scalar_tensor_tensor(neg_max[r], row_max[r], -1.0, neg_sink[:, hd], ALU.mult, ALU.min))
                dve.tensor_tensor(sink_exp[r], neg_max[r], sink[:, hd], ALU.add).then_inc(max_ready, 1)

            def row_sums(j):
                r = j % 3
                dve.wait_ge(p_ready, j + 1)
                step(dve.tensor_tensor(row_sum[r], row_sum[r], sink_exp[r], ALU.add))
                dve.reciprocal(row_sum[r], row_sum[r]).then_inc(rsum_ready, 1)

            def v_lo(j):
                hd = slice(64 * (j % 2), 64 * (j % 2) + 64)
                tok = slice((j // 2) * P, (j // 2 + 1) * P)
                dve.wait_ge(cat_hi_done, 4 + j + 1)
                dve.tensor_tensor(xn_lo[hd, 0:QH, tok], ps[hd, 6, :].rearrange("p (h q) -> p h q", q=P),
                                  f(xn_hi[hd, 0:QH, tok]), ALU.subtract).then_inc(cat_done, 1)

            scores(0)
            scores(1)
            row_sums(0)
            def pooled_add(j):
                dst = xres[:, j // 2, j % 2 * BANK:(j % 2 + 1) * BANK]
                dve.wait_ge(po_full, j + 1)
                dve.tensor_tensor(dst, ps[:, 7, :], dst, ALU.add).then_inc(po_added, 1)

            for j in range(NJ):
                pooled_add(j)
                if j >= 1:
                    v_lo(j - 1)
                if j + 2 < NJ:
                    scores(j + 2)
                if j + 1 < NJ:
                    row_sums(j + 1)
            v_lo(NJ - 1)
            dve.wait_ge(po_added, NJ)
            norm(1, two_outs)

            def gate_up():
                for k in range(2 * FB):
                    dve.wait_ge(pair_full, t.count("unit", 1))
                    dve.wait_ge(gate_done, t.count("gu", 1))
                    freed(dve.tensor_tensor(hid[k % 2][:, :], pair(t.n["unit"])[:, 1, :], gate[k % 2][:, :], ALU.mult))
                    t.add("gu")
                    dve.wait_ge(h_hi_done, t.count("gu"))
                    tok = slice((k % 2) * BANK, (k % 2 + 1) * BANK)
                    dve.tensor_tensor(h_lo[:, k // 2, tok], hid[k % 2][:, :], f(h_hi[:, k // 2, tok]), ALU.subtract)\
                        .then_inc(h_split, 1)

            def ffn():
                gate_up()
                with dve.Fori(0, ROUNDS - 1) as i:
                    t.enter(i, unit=2 * FB, gu=2 * FB, out=2 * NT)
                    for _ in range(2 * NT):
                        add_out()
                    gate_up()
                    t.leave(ROUNDS - 1)

            ffn()
            norm(2, two_outs)

            dtv, w1, eq, dA, dm, lu = D[0], D[3], D[5], D[6], D[6], D[7]

            def tiles(row):
                return row.unsqueeze(1).to_broadcast([P, NT, SH])

            freed(dve.tensor_copy(dtT[0:SH, :], unit()[0:SH, :]))
            dve.wait_ge(dt_full, 1)
            step(dve.tensor_tensor(dtv[:, :, :], ps[:, 4, 0:NT * SH].rearrange("p (c s) -> p c s", s=SH),
                                   tiles(dt_bias), ALU.add))
            dve.scalar_tensor_tensor(D[1][:, :, :], dtv[:, :, :], -1.0, dtv[:, :, :], ALU.mult, ALU.max).then_inc(dts_v, 1)
            dve.wait_ge(dts_a, 1)
            dve.tensor_scalar(w1[:, :, :], D[2][:, :, :], 1.0, None, ALU.add).then_inc(dts_v, 1)
            dve.wait_ge(dts_v, 2)
            dve.scalar_tensor_tensor(eq[:, :, :], w1[:, :, :], 1.0, D[2][:, :, :], ALU.is_equal, ALU.mult)
            step(dve.tensor_scalar(dm[:, :, :], w1[:, :, :], 1.0, 1e-30, ALU.subtract, ALU.max))
            dve.reciprocal(dm[:, :, :], dm[:, :, :])
            dve.wait_ge(dts_a, 3)
            step(dve.tensor_tensor(lu[:, :, :], D[4][:, :, :], D[2][:, :, :], ALU.mult))
            step(dve.tensor_tensor(lu[:, :, :], lu[:, :, :], dm[:, :, :], ALU.mult))
            step(dve.tensor_tensor(lu[:, :, :], lu[:, :, :], eq[:, :, :], ALU.add))
            step(dve.scalar_tensor_tensor(dtv[:, :, :], dtv[:, :, :], 0.0, lu[:, :, :], ALU.max, ALU.add))
            dve.scalar_tensor_tensor(dA[:, :, :], dtv[:, :, :], -1.0, tiles(exp_a), ALU.mult, ALU.mult).then_inc(dts_v, 1)

            def by_group(d):
                return d[:, :, :].rearrange("p c (g h) -> p g c h", h=HG)

            def group_major(ap):
                return ap.rearrange("p g (c h) -> p g c h", h=HG)

            dve.tensor_copy(group_major(gconst[:, :, GC_DT:GC_DT + NT * HG]), by_group(dtv))
            dve.wait_ge(dts_a, 4)
            dve.tensor_tensor(group_major(gda_lo[:, :, :]), by_group(dA), group_major(f(gda_hi[:, :, :])), ALU.subtract)\
                .then_inc(dts_v, 1)
            dve.wait_ge(sums_full, 1)
            acs = gconst[:, :, GC_ACS:GC_ACS + NT * HG]

            def flat_g(ap):
                return ap.rearrange("p (g k) -> p g k", g=G)
            dve.tensor_copy(acs, flat_g(ps[:, 5, 0:G * NT * HG]))
            step(dve.tensor_copy(D[7][:, :, :].rearrange("p c s -> p (c s)"), ps[:, 6, 0:G * NT * HG]))
            dve.tensor_tensor(flat_g(D[3][:, :, :].rearrange("p c s -> p (c s)")),
                              flat_g(D[7][:, :, :].rearrange("p c s -> p (c s)")), acs, ALU.subtract).then_inc(dts_v, 1)
            dve.wait_ge(dts_a, 6)

            def ssd_group(g, last=False):
                def group(ap):
                    return (ap[:, g:g + 1, :] if last else ap[:, bass.ds(g, 1), :]).rearrange("p g k -> p (g k)")
                dve.tensor_copy(gc[:, :], group(gconst))
                dve.tensor_copy(da_hi[:, :], group(f(gda_hi[:, :, :])))
                dve.tensor_copy(da_lo[:, :], group(f(gda_lo[:, :, :]))).then_inc(gc_ready, 1)
                t.add("group")
                dve.wait_ge(gc_ready, t.count("group"))
                for k in range(NCB):
                    full = unit()
                    dve.wait_ge(acc_ready, t.count("conv", 1))
                    for shift in range(1, CONV):
                        tap = GC_TAP + k * CONV + CONV - 1 - shift
                        ins = dve.scalar_tensor_tensor(acc[k % 2][:, shift:], full[:, 0:S - shift], gc[:, tap:tap + 1],
                                                       acc[k % 2][:, shift:], ALU.mult, ALU.add)
                        if shift < CONV - 1:
                            step(ins)
                        else:
                            freed(ins)
                    t.add("conv")

                def token_major(c):
                    dve.wait_ge(cb_full, t.count("chunk", c + 1))
                    if c == 0:
                        dve.wait_ge(silu_done, t.count("conv"))
                    dve.tensor_tensor(cbm[c % 2][:, :], ps[:, CB, 0:P], f(tri[:, :]), ALU.mult)
                    if c:
                        dve.wait_ge(states_full, t.count("chunk", c))
                    dve.tensor_copy(btok[:, :], ps[:, CB, P:2 * P]).then_inc(cb_freed, 1)
                    dve.wait_ge(xsT_full, t.count("chunk", c + 1))
                    if c >= 2:
                        dve.wait_ge(ydiag_full, t.count("chunk", c - 1))
                    dve.tensor_tensor(xdt[c % 2][:, :].rearrange("p (h d) -> p h d", d=PH),
                                      ps[:, XS, :].rearrange("p (h d) -> p h d", d=PH),
                                      gc[:, GC_DT + c * HG:GC_DT + (c + 1) * HG].unsqueeze(2).to_broadcast([P, HG, PH]),
                                      ALU.mult).then_inc(xdt_ready, 1)

                def gate_first_half(b):
                    dve.wait_ge(z_done, t.count("z", BG + b + 1))
                    dve.tensor_tensor(yx[:, b, 0:BANK], ps[:, Z_BANK, :], yx[:, b, 0:BANK], ALU.mult).then_inc(z_gated, 1)

                token_major(0)
                for c in range(NT):
                    tok = slice(c * P, (c + 1) * P)
                    if c:
                        dve.wait_ge(ydiag_full, t.count("chunk", c))
                    for hf in range(2):
                        dve.wait_ge(dec_ready, t.count("half", 2 * c + hf + 1))
                        if hf == 0:
                            dve.wait_ge(cb_freed, t.count("chunk", c + 1))
                        dve.tensor_tensor(mdec[:, 4 * hf:4 * hf + 4, :], ps[:, DECAY + hf, :].rearrange("p (h l) -> p h l", l=P),
                                          cbm[c % 2][:, :].unsqueeze(1).to_broadcast([P, 4, P]), ALU.mult)\
                            .then_inc(m_ready, 1)
                    if c + 1 < NT:
                        token_major(c + 1)
                    if BG <= c < NT - 1:
                        if c == BG:
                            dve.wait_ge(y_ready, t.count("chunk", BG))
                        gate_first_half(c - BG)
                    dve.wait_ge(states_full, t.count("chunk", c + 1))
                    if c:
                        dve.wait_ge(decayed_ready, t.count("carry", c))
                        dve.wait_ge(yoff_full, t.count("carry", c))
                        dve.tensor_tensor(state[:, :], ps[:, STATES, :], decayed[:, :], ALU.add).then_inc(state_ready, 1)
                    else:
                        dve.tensor_copy(state[:, :], ps[:, STATES, :]).then_inc(state_ready, 1)
                    dve.wait_ge(e_ready, t.count("half", 2 * c + 2))
                    e = eacs[c % 2]
                    e2 = e[:, :, :].rearrange("p b l -> p (b l)")
                    if c:
                        dve.tensor_tensor(e2, ps[:, YOFF, :], e2, ALU.mult).then_inc(yoff_read, 1)
                        dve.wait_ge(yoff_read, t.count("chunk", c + 1))
                        dve.wait_ge(ydiag_full, t.count("chunk", c + 1))
                        step(dve.tensor_tensor(e2, ps[:, YDIAG, :], e2, ALU.add))
                    else:
                        dve.wait_ge(ydiag_full, t.count("chunk", c + 1))
                        dve.tensor_copy(e2, ps[:, YDIAG, :]).then_inc(yoff_read, 1)
                        dve.wait_ge(yoff_read, t.count("chunk", c + 1))
                    for b in range(BG):
                        d = gc[:, GC_D + b:GC_D + b + 1]
                        ins = dve.scalar_tensor_tensor(yx[:, b, tok], yx[:, b, tok], d, e[:, b, :], ALU.mult, ALU.add)
                    ins.then_inc(y_ready, 1)
                t.add("chunk", NT)
                t.add("half", 2 * NT)
                t.add("carry", NT - 1)

                def lo(b, h):
                    half = slice(h * BANK, (h + 1) * BANK)
                    dve.wait_ge(y_hi_done, t.count("z", BG * h + b + 1))
                    dve.scalar_tensor_tensor(y_lo[:, b, half], yx[:, b, half], gc[:, GC_NW + b:GC_NW + b + 1],
                                             f(y_hi[:, b, half]), ALU.mult, ALU.subtract).then_inc(y_split, 1)

                def gate_second_half(b):
                    dve.tensor_tensor(yx[:, b, BANK:], zs[b][:, :], yx[:, b, BANK:], ALU.mult).then_inc(z_gated, 1)

                def reciprocal_rms(h):
                    dve.wait_ge(rms_rooted, t.count("rms", 1))
                    dve.reciprocal(rms[:, 4 * h:4 * h + 4], rms[:, 4 * h:4 * h + 4]).then_inc(rms_ready, 1)
                    t.add("rms")
                    dve.wait_ge(rms_ready, t.count("rms"))

                def outs(tt):
                    if tt == 0:
                        reciprocal_rms(0)
                    add_out(rms)
                    add_out(rms)
                    if tt < 2:
                        lo(2 * tt, 1)
                        lo(2 * tt + 1, 1)
                    if tt == 1:
                        reciprocal_rms(1)

                for b in range(BG - 1):
                    lo(b, 0)
                gate_first_half(BG - 1)
                dve.wait_ge(y_ready, t.count("chunk"))
                gate_second_half(0)
                lo(BG - 1, 0)
                for b in range(1, BG):
                    gate_second_half(b)
                if last:
                    norm(3, outs, xn3, norm_w3)
                else:
                    for tt in range(NT):
                        outs(tt)
                t.add("z", 2 * BG)

            dve_loop = dict(unit=NCB, conv=NCB, z=2 * BG, chunk=NT, half=2 * NT, out=2 * NT, carry=NT - 1, group=1, rms=2)
            with dve.Fori(0, G - 1) as g:
                t.enter(g, step=(CONV - 2) * NCB + NT - 1, **dve_loop)
                ssd_group(g)
                t.leave(G - 1)
            ssd_group(G - 1, True)

            ffn()
            for tt in range(NT):
                add_out()
                add_out()
                if tt >= 1:
                    if tt >= 3:
                        dve.wait_ge(stored[(tt - 1) % 2], 16 * ((tt - 1) // 2))
                    normed(4, tt - 1, xn[(tt - 1) % 2]).then_inc(final_ready, 1)
            dve.wait_ge(stored[(NT - 1) % 2], 16 * ((NT - 1) // 2))
            normed(4, NT - 1, xn[(NT - 1) % 2]).then_inc(final_ready, 1)


INPUTS = ["x", "mix_norm_w", "ap_w_in", "ap_sinks", "pool_w", "pool_scale", "ap_w_out", "ssd_w_in", "ssd_conv_w",
          "ssd_conv_b", "ssd_dt_bias", "ssd_A_log", "ssd_D", "ssd_norm_w", "ssd_w_out", "ffn_norm_w", "w_gate",
          "w_up", "w_down", "final_norm_w"]


def kernel(**inputs):
    import numpy as np
    import concourse.bacc as bacc
    from concourse.bass_utils import run_bass_kernel_spmd

    nc = bacc.Bacc("TRN2", target_bir_lowering=False, num_devices=1)
    arrays, args = {}, []
    for name in INPUTS:
        a = np.ascontiguousarray(inputs[name])
        arrays[f"in_{name}"] = a
        args.append(nc.dram_tensor(f"in_{name}", a.shape, mybir.dt.from_np(a.dtype), kind="ExternalInput").ap())
    out = nc.dram_tensor("out", inputs["x"].shape, F32, kind="ExternalOutput").ap()
    trunk(nc, *args, out)
    r = run_bass_kernel_spmd(nc, [arrays], core_ids=[0])
    return r.results[0]["out"]
```
